# Optimizing a Trainium2 kernel written in Bass

```python
import math
import jax, jax.numpy as jnp
from jax import lax
import numpy as np

D_MODEL = 2048
BATCH = 1
SEQ = 256
DEPTH = 1

CHUNK = 64
Q_BLOCK = 128

MLA_HEADS = 8
MLA_Q_LORA = 512
MLA_KV_LORA = 256
MLA_NOPE = 128
MLA_ROPE = 64
MLA_V = 128
ROPE_THETA = 10000.0

FOX_HEADS = 8
FOX_HEAD_DIM = 128

D_FF = 4 * D_MODEL

EPS = 1e-6

OFF_CQ = 0
OFF_CKV = OFF_CQ + MLA_Q_LORA
OFF_KR = OFF_CKV + MLA_KV_LORA
OFF_FQ = OFF_KR + MLA_ROPE
OFF_FK = OFF_FQ + FOX_HEADS * FOX_HEAD_DIM
OFF_FV = OFF_FK + FOX_HEADS * FOX_HEAD_DIM
OFF_FF = OFF_FV + FOX_HEADS * FOX_HEAD_DIM
OFF_G = OFF_FF + FOX_HEADS
D_IN = OFF_G + 2 * D_MODEL

kernel_name = "hybrid_mla_fox_gated_block"

def rmsnorm(x, g):
    xf = x.astype(jnp.float32)
    y = xf * lax.rsqrt(jnp.mean(xf * xf, axis=-1, keepdims=True) + EPS)
    return (y * g.astype(jnp.float32)).astype(x.dtype)

def rope_tables(seq_len):
    pos = jnp.arange(seq_len, dtype=jnp.float32)
    inv = 1.0 / (ROPE_THETA ** (jnp.arange(0, MLA_ROPE, 2, dtype=jnp.float32) / MLA_ROPE))
    ang = pos[:, None] * inv[None, :]
    return jnp.cos(ang), jnp.sin(ang)

def apply_rope(x, cos, sin):
    half = x.shape[-1] // 2
    x1, x2 = x[..., :half], x[..., half:]
    c = cos.astype(x.dtype)
    s = sin.astype(x.dtype)
    return jnp.concatenate([x1 * c - x2 * s, x1 * s + x2 * c], axis=-1)

def block_attention(q, k, v, scale, chunk_causal, cum=None):
    B, H, S, Dq = q.shape
    Dv = v.shape[-1]
    nb = S // Q_BLOCK
    qb = q.reshape(B, H, nb, Q_BLOCK, Dq).transpose(2, 0, 1, 3, 4)
    k_pos = jnp.arange(S)
    xs = (jnp.arange(nb), qb)
    if cum is not None:
        cb = cum.reshape(B, H, nb, Q_BLOCK).transpose(2, 0, 1, 3)
        xs = xs + (cb,)

    def one_block(args):
        i, q_blk = args[0], args[1]
        s = jnp.einsum('bhqd,bhkd->bhqk', q_blk, k,
                       preferred_element_type=jnp.float32) * scale
        q_pos = i * Q_BLOCK + jnp.arange(Q_BLOCK)
        if chunk_causal:
            mask = (k_pos // CHUNK)[None, :] <= (q_pos // CHUNK)[:, None]
        else:
            mask = k_pos[None, :] <= q_pos[:, None]
        if cum is not None:
            c_blk = args[2]
            s = s + c_blk[..., :, None] - cum[:, :, None, :]
        s = jnp.where(mask, s, -jnp.inf)
        p = jax.nn.softmax(s, axis=-1)
        return jnp.einsum('bhqk,bhkd->bhqd', p.astype(v.dtype), v)

    out = lax.map(one_block, xs)
    return out.transpose(1, 2, 0, 3, 4).reshape(B, H, S, Dv)

def mla_branch(proj, q_norm, w_uq, kv_norm, w_ukv, cos, sin):
    B, S, _ = proj.shape
    cq = rmsnorm(proj[..., OFF_CQ:OFF_CKV], q_norm)
    q = (cq @ w_uq).reshape(B, S, MLA_HEADS, MLA_NOPE + MLA_ROPE).transpose(0, 2, 1, 3)
    ckv = rmsnorm(proj[..., OFF_CKV:OFF_KR], kv_norm)
    kv = (ckv @ w_ukv).reshape(B, S, MLA_HEADS, MLA_NOPE + MLA_V).transpose(0, 2, 1, 3)
    k_nope, v = kv[..., :MLA_NOPE], kv[..., MLA_NOPE:]
    k_rope = apply_rope(proj[:, None, :, OFF_KR:OFF_FQ], cos, sin)
    q = jnp.concatenate([q[..., :MLA_NOPE], apply_rope(q[..., MLA_NOPE:], cos, sin)], axis=-1)
    k = jnp.concatenate(
        [k_nope, jnp.broadcast_to(k_rope, (B, MLA_HEADS, S, MLA_ROPE))], axis=-1)
    o = block_attention(q, k, v, 1.0 / math.sqrt(MLA_NOPE + MLA_ROPE), chunk_causal=True)
    return o.transpose(0, 2, 1, 3).reshape(B, S, MLA_HEADS * MLA_V)

def fox_branch(proj, f_bias):
    B, S, _ = proj.shape

    def heads(a):
        return a.reshape(B, S, FOX_HEADS, FOX_HEAD_DIM).transpose(0, 2, 1, 3)

    q = heads(proj[..., OFF_FQ:OFF_FK])
    k = heads(proj[..., OFF_FK:OFF_FV])
    v = heads(proj[..., OFF_FV:OFF_FF])
    logf = jax.nn.log_sigmoid((proj[..., OFF_FF:OFF_G] + f_bias).astype(jnp.float32))
    cum = jnp.cumsum(logf, axis=1).transpose(0, 2, 1)
    o = block_attention(q, k, v, 1.0 / math.sqrt(FOX_HEAD_DIM), chunk_causal=False, cum=cum)
    return o.transpose(0, 2, 1, 3).reshape(B, S, FOX_HEADS * FOX_HEAD_DIM)

def setup_inputs(seed: int = 0) -> dict:
    key = jax.random.key(seed)
    ks = jax.random.split(key, 20)
    f32 = jnp.float32

    def w(k, shape, fan_in):
        return jax.random.normal(k, shape, f32) * (fan_in ** -0.5)

    def gain(k, shape):
        return 1.0 + 0.02 * jax.random.normal(k, shape, f32)

    return {
        "x": jax.random.normal(ks[0], (BATCH, SEQ, D_MODEL), f32),
        "attn_norm": gain(ks[1], (DEPTH, D_MODEL)),
        "w_in": w(ks[2], (DEPTH, D_MODEL, D_IN), D_MODEL),
        "fox_f_bias": jax.random.uniform(ks[3], (DEPTH, FOX_HEADS), f32, 1.0, 6.0),
        "q_norm": gain(ks[4], (DEPTH, MLA_Q_LORA)),
        "w_uq": w(ks[5], (DEPTH, MLA_Q_LORA, MLA_HEADS * (MLA_NOPE + MLA_ROPE)), MLA_Q_LORA),
        "kv_norm": gain(ks[6], (DEPTH, MLA_KV_LORA)),
        "w_ukv": w(ks[7], (DEPTH, MLA_KV_LORA, MLA_HEADS * (MLA_NOPE + MLA_V)), MLA_KV_LORA),
        "w_mla_branch": w(ks[8], (DEPTH, MLA_HEADS * MLA_V, D_MODEL), MLA_HEADS * MLA_V),
        "w_fox_branch": w(ks[9], (DEPTH, FOX_HEADS * FOX_HEAD_DIM, D_MODEL), FOX_HEADS * FOX_HEAD_DIM),
        "w_out": w(ks[10], (DEPTH, D_MODEL, D_MODEL), D_MODEL),
        "mlp_norm": gain(ks[11], (DEPTH, D_MODEL)),
        "w_up": w(ks[12], (DEPTH, D_MODEL, D_FF), D_MODEL),
        "w_down": w(ks[13], (DEPTH, D_FF, D_MODEL), D_FF),
        "final_norm": gain(ks[14], (D_MODEL,)),
    }

def reference(x, attn_norm, w_in, fox_f_bias, q_norm, w_uq, kv_norm, w_ukv,
              w_mla_branch, w_fox_branch, w_out, mlp_norm, w_up, w_down, final_norm):
    S = x.shape[1]
    cos, sin = rope_tables(S)
    h = x
    for l in range(DEPTH):
        xn = rmsnorm(h, attn_norm[l])
        proj = xn @ w_in[l]
        y_mla = mla_branch(proj, q_norm[l], w_uq[l], kv_norm[l], w_ukv[l], cos, sin) @ w_mla_branch[l]
        y_fox = fox_branch(proj, fox_f_bias[l]) @ w_fox_branch[l]
        gates = jax.nn.sigmoid(proj[..., OFF_G:])
        g_mla, g_fox = gates[..., :D_MODEL], gates[..., D_MODEL:]
        h = h + (g_mla * y_mla + g_fox * y_fox) @ w_out[l]
        hn = rmsnorm(h, mlp_norm[l])
        u = jnp.square(jax.nn.relu(hn @ w_up[l]))
        h = h + u @ w_down[l]
    return rmsnorm(h, final_norm)


_drawn_inputs = setup_inputs


def setup_inputs(seed=0):
    import zlib

    import numpy as np

    out = dict(_drawn_inputs(seed))
    spreads = {}
    factors = {'attn_norm': 8.0, 'q_norm': 8.0, 'kv_norm': 8.0, 'mlp_norm': 9.471, 'final_norm': 7.739}
    for name, (base, spread) in spreads.items():
        noise = np.random.default_rng([zlib.crc32(name.encode()), seed]).standard_normal(out[name].shape)
        drawn = base * np.exp(spread * noise) if base else spread * noise
        out[name] = __import__('jax').numpy.asarray(drawn.astype(out[name].dtype))
    for name, factor in factors.items():
        out[name] = (out[name] * factor).astype(out[name].dtype)
    return out
```

```python
import math
from contextlib import ExitStack

import numpy as np
import concourse.bass as bass
from concourse import mybir

F32 = mybir.dt.float32
F32R = mybir.dt.float32r
ALU = mybir.AluOpType
ACT = mybir.ActivationFunctionType
AX = mybir.AxisListType

P = 128
D = 2048
T = 256
TB = T // P
CHUNK = 64
HEADS = 8
DH = 128
ROPE = 64
Q_LORA, KV_LORA = 512, 256
D_FF = 4 * D
ROPE_THETA = 10000.0
EPS = 1e-6
KT = D // P
KQ, KKV = Q_LORA // P, KV_LORA // P

OFF_CKV = Q_LORA
OFF_KR = OFF_CKV + KV_LORA
OFF_FQ = OFF_KR + ROPE
OFF_FK = OFF_FQ + HEADS * DH
OFF_FV = OFF_FK + HEADS * DH
OFF_FF = OFF_FV + HEADS * DH
OFF_G = OFF_FF + HEADS

SLABS, COLS = 4, 256
UNIT = SLABS * COLS
RING = 4
MLP_PARTS = 2
FF_GROUPS = D_FF // COLS // MLP_PARTS

FOX_SCALE = 1.0 / math.sqrt(DH)
MLA_SCALE = 1.0 / math.sqrt(DH + ROPE)
MASKED = -3.0e38

FF_A, FF_B = 64, 96


class Stage:
    def __init__(self, name, groups, units):
        self.name, self.groups, self.units = name, groups, units
        self.g0 = self.u0 = 0


def make_stages():
    stages = [
        Stage("cq", Q_LORA // COLS, KT // SLABS),
        Stage("ckv", KV_LORA // COLS, KT // SLABS),
        Stage("krff", 1, KT // SLABS // 2),
        Stage("fq", HEADS * DH // COLS, KT // SLABS),
        Stage("fk", HEADS * DH // COLS, KT // SLABS),
        Stage("fv", HEADS * DH // COLS, KT // SLABS),
        Stage("gates", 2 * D // COLS, KT // SLABS),
        Stage("uq_nope", HEADS * DH // COLS, KQ // SLABS),
        Stage("uq_rope", HEADS * ROPE // COLS, KQ // SLABS),
        Stage("ukv_k", HEADS * DH // COLS, 0.5),
        Stage("ukv_v", HEADS * DH // COLS, 0.5),
        Stage("y_fox", D // COLS, HEADS // SLABS),
        Stage("y_mla", D // COLS, HEADS // SLABS),
        Stage("w_out", D // COLS, KT // SLABS),
    ]
    for part in range(MLP_PARTS):
        stages.append(Stage(f"up{part}", FF_GROUPS, KT // SLABS))
        stages.append(Stage(f"down{part}", D // COLS, D_FF // P // MLP_PARTS // SLABS))
    g = u = 0
    for s in stages:
        s.g0, s.u0 = g, u
        g += s.groups
        u += int(s.groups * s.units)
    return stages, g, u


STAGES, N_GROUPS, N_UNITS = make_stages()
S = {s.name: s for s in STAGES}
assert N_UNITS % RING == 0

C_IDENT = 0
C_MASK_FOX = C_IDENT + P
C_MASK_MLA = C_MASK_FOX + 3 * P
C_COS = C_MASK_MLA + 3 * P
C_SIN = C_COS + T
C_ONES = C_SIN + T
C_LEFT = C_ONES + T
C_RIGHT_M = C_LEFT + 2
C_RIGHT_N = C_RIGHT_M + HEADS
C_EPS = C_RIGHT_N + HEADS
C_COUNT = C_EPS + 1

G_ATTN = 0
G_Q = G_ATTN + KT
G_KV = G_Q + KQ
G_MLP = G_KV + KKV
G_FINAL = G_MLP + KT
G_FBIAS = G_FINAL + KT
G_COUNT = G_FBIAS + 1


def constants():
    c = np.zeros((P, C_COUNT), np.float32)
    p = np.arange(P)
    c[:, C_IDENT:C_IDENT + P] = np.eye(P)
    for col, keep in ((C_MASK_FOX, p[None, :] <= p[:, None]),
                      (C_MASK_MLA, p[None, :] // CHUNK <= p[:, None] // CHUNK)):
        diagonal = np.where(keep, 0.0, MASKED)
        c[:, col:col + P] = diagonal
        c[:, col + 2 * P:col + 3 * P] = diagonal
    half = ROPE // 2
    inv = np.float32(1.0) / np.power(np.float32(ROPE_THETA),
                                     np.arange(0, ROPE, 2, dtype=np.float32) / np.float32(ROPE))
    angle = (inv[p % half][:, None] * np.arange(T, dtype=np.float32)[None, :]).astype(np.float32)
    c[:, C_COS:C_COS + T] = np.cos(angle)
    c[:, C_SIN:C_SIN + T] = np.where(p % ROPE < half, -1.0, 1.0)[:, None] * np.sin(angle)
    c[:, C_ONES:C_ONES + T] = 1.0
    c[FF_B:FF_B + HEADS, C_LEFT] = 1.0
    c[FF_A:FF_A + HEADS, C_LEFT + 1] = 1.0
    for h in range(HEADS):
        c[FF_A + h, C_RIGHT_M + h] = -1.0
        c[FF_B + h, C_RIGHT_N + h] = 1.0
    c[:, C_EPS] = EPS
    return c


def program(nc, stream, x_t, consts, gains, out_t):
    sbuf0 = (nc.sbuf_base + 511) // 512 * 512
    kib = 1024

    def at(name, offset, *shape, dt=F32):
        return nc.alloc_sbuf_tensor_at(name, [P, *shape], dt, offset=sbuf0 + offset)

    raw = at("raw", 0, RING, SLABS, COLS)
    hl = at("hl", 16 * kib, RING, SLABS, 2, COLS, dt=F32R)
    H = 48 * kib
    o_fox = at("o_fox", H, HEADS, 2, T, dt=F32R)
    resid = at("resid", H, KT, T)
    o = H + 16 * kib
    cst = at("cst", o, C_COUNT)
    gain = at("gain", o + 8 * kib, G_COUNT)
    cols = at("cols", o + 8 * kib + 512, 4, 4)
    part = at("part", o + 9 * kib, 2, 2, T)
    zsum = at("zsum", o + 13 * kib, 2, T)
    std = at("std", o + 15 * kib, 2, T)
    rstd = at("rstd", o + 17 * kib, 2, T)
    prob = at("prob", o + 19 * kib, 2, 3, P)
    prob_t = at("prob_t", o + 22 * kib, 2, 3, P)
    full = at("full", o + 19 * kib, 2, T)
    assert C_COUNT * 4 <= 8 * kib and G_COUNT * 4 <= 512
    A = o + 25 * kib
    x_hl = at("x_hl", A, KT, 2, T, dt=F32R)
    qn = at("qn", A, HEADS, T)
    kn = at("kn", A + 8 * kib, HEADS, T)
    v_mla = at("v_mla", A + 16 * kib, TB, HEADS * DH)
    qr = at("qr", A + 24 * kib, HEADS // 2, T)
    m_hl = at("m_hl", A, KT, 2, T, dt=F32R)
    B = A + 32 * kib
    fq = at("fq", B, HEADS, T)
    fk = at("fk", B + 8 * kib, HEADS, T)
    v_fox = at("v_fox", B + 16 * kib, TB, HEADS * DH)
    cq_hl = at("cq_hl", B + 24 * kib, KQ, 2, T, dt=F32R)
    o_mla = at("o_mla", B, HEADS, 2, T, dt=F32R)
    qr_z = at("qr_z", B + 16 * kib, 2, T)
    qr_swap = at("qr_swap", B + 18 * kib, 2, T)
    qr_sin = at("qr_sin", B + 20 * kib, 2, T)
    sq = at("sq", B, 2, 2, T)
    xn = at("xn", B + 4 * kib, KT, T)
    u_hl = at("u_hl", A, D_FF // P // MLP_PARTS, 2, T, dt=F32R)
    final = at("final", A, KT, T)
    C = B + 32 * kib
    x_in = at("x_in", C, KT, T)
    gate = at("gate", C, 2 * KT, T)
    cq_z = at("cq_z", C, KQ, T)
    ckv_z = at("ckv_z", C + 4 * kib, KKV, T)
    cq_sq = at("cq_sq", C + 6 * kib, KQ, T)
    ckv_sq = at("ckv_sq", C + 10 * kib, KKV, T)
    cq_n = at("cq_n", C + 12 * kib, KQ, T)
    ckv_n = at("ckv_n", C + 16 * kib, KKV, T)
    kr_z = at("kr_z", C + 18 * kib, T)
    kr_swap = at("kr_swap", C + 19 * kib, T)
    ff_a = at("ff_a", C + 20 * kib, T)
    ff_b = at("ff_b", C + 21 * kib, T)
    ff_c = at("ff_c", C + 22 * kib, T)
    last_n = at("last_n", C, KT, T)
    hn_hl = at("hn_hl", C, KT, 2, T, dt=F32R)
    E = C + 32 * kib
    ckv_hl = at("ckv_hl", E, KKV, 2, T, dt=F32R)
    k_rope = at("k_rope", E + 4 * kib, 2, T)
    left = at("left", E + 6 * kib, T)
    right = at("right", E + 7 * kib, 2, T)
    assert sbuf0 + E + 9 * kib <= nc.sbuf_usable_end

    ctx = ExitStack()
    with ctx:
        sem = lambda name: ctx.enter_context(nc.semaphore(name))
        bank = ctx.enter_context(nc.psum_tensor("bank", [P, 8, 512], F32))

        unit_loaded = [sem(f"unit_loaded{i}") for i in range(RING)]
        unit_hi = sem("unit_hi")
        unit_split = sem("unit_split")
        halves_used = sem("halves_used")
        group_low = sem("group_low")
        group_out = sem("group_out")
        consts_in = sem("consts_in")
        x_loaded = [sem(f"x_loaded{i}") for i in range(4)]
        resid_in = sem("resid_in")
        zeroed = sem("zeroed")
        squares = sem("squares")
        squares_used = sem("squares_used")
        std_done = sem("std_done")
        normed = sem("normed")
        norm_hi = sem("norm_hi")
        norm_split = sem("norm_split")
        rope_ready = sem("rope_ready")
        weighted = sem("weighted")
        ff_exp = sem("ff_exp")
        ff_ln = sem("ff_ln")
        ff_abs = sem("ff_abs")
        bias_ready = sem("bias_ready")
        scored = sem("scored")
        max_ready = sem("max_ready")
        exp_done = sem("exp_done")
        prob_ready = sem("prob_ready")
        transposed = sem("transposed")
        prob_t_ready = sem("prob_t_ready")
        mixed = sem("mixed")
        o_hi = sem("o_hi")
        o_split = sem("o_split")
        gate_done = sem("gate_done")
        full_ready = sem("full_ready")
        full_hi = sem("full_hi")
        full_split = sem("full_split")
        resid_done = sem("resid_done")
        final_done = sem("final_done")
        stored = sem("stored")
        vec_step = sem("vec_step")

        block = ctx.enter_context(nc.Block())

        FULL0 = {"y_mla": 0}
        for i in range(MLP_PARTS):
            FULL0[f"up{i}"] = S["y_mla"].groups + i * FF_GROUPS
        X_NORM, Q_NORM, KV_NORM, MLP_NORM, LAST_NORM = range(5)
        SQ0 = {X_NORM: 0, Q_NORM: KT // 2, KV_NORM: KT // 2 + 1, MLP_NORM: KT // 2 + 2,
               LAST_NORM: KT + 2}
        NORMED0 = {X_NORM: 0, Q_NORM: KT // 2, KV_NORM: KT // 2 + KQ // 2,
                   MLP_NORM: KT // 2 + KQ // 2 + KKV // 2,
                   LAST_NORM: KT + KQ // 2 + KKV // 2}
        SPLIT0 = {X_NORM: 0, Q_NORM: KT, KV_NORM: KT + KQ, MLP_NORM: KT + KQ + KKV}

        def run(eng, stage, first, last, body):
            if 2 * stage.units % RING:
                for g in range(first, last):
                    body(g, g)
                return
            if (last - first) % 2:
                body(first, first)
                first += 1
            if last - first == 2:
                body(first, first)
                body(first + 1, first + 1)
            elif last > first:
                with eng.Fori(0, (last - first) // 2) as i:
                    body(i * 2 + first, first)
                    body(i * 2 + (first + 1), first + 1)

        def slots_of(stage, g, j):
            if stage.units == 0.5:
                return [(stage.u0 + g // 2, (stage.u0 + j // 2) % RING)]
            n = stage.units
            return [(g * n + (stage.u0 + k), (stage.u0 + j * n + k) % RING) for k in range(n)]

        def pair_of(stage, j):
            return 2 * ((stage.g0 + j) % 2)

        def halves_until(stage, g):
            halves = int(2 * stage.units)
            return g * halves + (int(2 * stage.u0) + halves)

        @block.sync
        def _(sp):
            for n in range(RING):
                sp.dma_start(raw[:, n], stream[n]).then_inc(unit_loaded[n], 16)
            with sp.Fori(1, N_UNITS // RING) as turn:
                for k in range(RING):
                    sp.wait_ge(unit_split, turn * RING + (k + 1 - RING))
                    sp.dma_start(raw[:, k], stream[bass.ds(turn * RING + k, 1)].rearrange("a p s c -> p (a s) c"))\
                      .then_inc(unit_loaded[k], 16)
            for i in range(4):
                sp.wait_ge(final_done, 4 * (i + 1))
                sp.dma_start(out_t[:, 4 * i:4 * i + 4], final[:, 4 * i:4 * i + 4]).then_inc(stored, 16)
            sp.wait_ge(stored, 64)

        @block.gpsimd
        def _(pool):
            nc.gpsimd.memset(k_rope[:], 0.0).then_inc(zeroed, 1)
            nc.gpsimd.memset(left[:], 0.0).then_inc(zeroed, 1)
            nc.gpsimd.memset(right[:], 0.0).then_inc(zeroed, 1)
            pool.wait_ge(halves_used, halves_until(S["y_fox"], S["y_fox"].groups - 1))
            pool.dma_start(resid[:], x_t).then_inc(resid_in, 16)

        @block.tensor
        def _(pe):
            def norm_sum(norm, b, pieces):
                for j, tiles in enumerate(pieces):
                    pe.wait_ge(squares, SQ0[norm] + j + 1)
                    for i, tile in enumerate(tiles):
                        last = nc.tensor.matmul(bank[:, b, 0:T], cst[:, C_ONES:C_ONES + P], tile,
                                                start=(j == 0 and i == 0),
                                                stop=(j == len(pieces) - 1 and i == len(tiles) - 1))
                    last.then_inc(squares_used, 1)

            def group(stage, g, j, moving, k_tiles, values=False, narrow=False, ready=None):
                b0 = pair_of(stage, j)
                if stage.g0 + j >= 2:
                    pe.wait_ge(group_out, g + (stage.g0 - 1))
                k = 0
                units = slots_of(stage, g, j)
                for ui, (n, slot) in enumerate(units):
                    pe.wait_ge(unit_split, n + 1)
                    slabs = range(SLABS)
                    if stage.units == 0.5:
                        slabs = range(2 * (j % 2), 2 * (j % 2) + 2)
                    if ready is not None:
                        ready(ui)
                    for s in slabs:
                        for sub in range(2 if narrow else 1):
                            x = moving(k)
                            first, end = k == 0, k == k_tiles - 1
                            for b in range(1 if narrow else 2):
                                ps = bank[:, b0 + b]
                                at_ = P * (sub if narrow else b)
                                if values:
                                    tok = slice(b * P, b * P + P)
                                    nc.tensor.matmul(ps, x[:, 0, tok], hl[:, slot, s].rearrange("p h c -> p (h c)"),
                                                     start=first, stop=False)
                                    last = nc.tensor.matmul(ps[:, T:], x[:, 1, tok], hl[:, slot, s, 0],
                                                            start=False, stop=end)
                                else:
                                    nc.tensor.matmul(ps, hl[:, slot, s, 0, at_:at_ + P],
                                                     x.rearrange("p h t -> p (h t)"), start=first, stop=False)
                                    last = nc.tensor.matmul(ps[:, T:], hl[:, slot, s, 1, at_:at_ + P], x[:, 0],
                                                            start=False, stop=end)
                            k += 1
                        if s % 2:
                            last.then_inc(halves_used, 1)
                assert k == k_tiles

            def norm_ready(norm, per_unit):
                return lambda ui: pe.wait_ge(norm_split, SPLIT0[norm] + per_unit * (ui + 1))

            def plain(stage, tile, k_tiles, first=0, last=None, **kw):
                last = stage.groups if last is None else last
                def body(g, j):
                    group(stage, g, j, lambda k: tile[:, k], k_tiles, **kw)
                run(pe, stage, first, last, body)

            def scores(i, branch):
                done = i + 4 * (branch == "mla")
                if done:
                    pe.wait_ge(max_ready, done)
                if branch == "fox":
                    pe.wait_ge(bias_ready, i + 1)
                for hh in range(2):
                    h = 2 * i + hh
                    for qs, ks, c0 in ((slice(0, P), slice(0, P), 0), (slice(P, T), slice(0, T), P)):
                        dst = bank[:, 4 + hh, c0:c0 + ks.stop]
                        if branch == "fox":
                            nc.tensor.matmul(dst, fq[:, h, qs], fk[:, h, ks], start=True, stop=False)
                            last = nc.tensor.matmul(dst, left[:, qs], right[:, hh, ks], start=False, stop=True)
                        else:
                            nc.tensor.matmul(dst, qn[:, h, qs], kn[:, h, ks], start=True, stop=False)
                            last = nc.tensor.matmul(dst, qr[:, i, qs], k_rope[:, hh, ks], start=False, stop=True)
                last.then_inc(scored, 1)

            def transposes(i, branch):
                done = i + 4 * (branch == "mla")
                pe.wait_ge(prob_ready, done + 1)
                if done:
                    pe.wait_ge(o_split, done)
                for hh in range(2):
                    for piece in range(3):
                        last = nc.tensor.transpose(bank[:, 6 + hh, piece * P:piece * P + P],
                                                   prob[:, hh, piece], cst[:, C_IDENT:C_IDENT + P])
                last.then_inc(transposed, 1)

            def mix(i, branch):
                v = v_fox if branch == "fox" else v_mla
                pe.wait_ge(prob_t_ready, i + 4 * (branch == "mla") + 1)
                for hh in range(2):
                    cs = slice((2 * i + hh) * DH, (2 * i + hh + 1) * DH)
                    nc.tensor.matmul(bank[:, 6, hh * T:hh * T + T], v[:, 0, cs],
                                     prob_t[:, hh, 0:2].rearrange("p b q -> p (b q)"), start=True, stop=False)
                    last = nc.tensor.matmul(bank[:, 6, hh * T + P:hh * T + T], v[:, 1, cs],
                                            prob_t[:, hh, 2], start=False, stop=True)
                last.then_inc(mixed, 1)

            def attend(stage, tile, k_tiles, branch, **kw):
                scores(0, branch)
                for g in range(8):
                    group(stage, g, g, lambda k: tile[:, k], k_tiles, **kw)
                    if g % 2 == 0:
                        transposes(g // 2, branch)
                        if g < 6:
                            scores(g // 2 + 1, branch)
                    else:
                        mix(g // 2, branch)

            pe.wait_ge(consts_in, 32)
            norm_sum(X_NORM, 4, [[sq[:, j % 2, 0], sq[:, j % 2, 1]] for j in range(KT // 2)])
            plain(S["cq"], x_hl, KT, ready=norm_ready(X_NORM, SLABS))
            plain(S["ckv"], x_hl, KT)
            plain(S["krff"], x_hl, KT, narrow=True)
            plain(S["fq"], x_hl, KT, last=1)
            norm_sum(Q_NORM, 4, [[cq_sq[:, k] for k in range(KQ)]])
            norm_sum(KV_NORM, 5, [[ckv_sq[:, k] for k in range(KKV)]])
            plain(S["fq"], x_hl, KT, first=1)
            plain(S["fk"], x_hl, KT)
            plain(S["fv"], x_hl, KT, values=True)
            pe.wait_ge(group_out, S["fv"].g0 + S["fv"].groups)
            attend(S["gates"], x_hl, KT, "fox")
            plain(S["gates"], x_hl, KT, first=8)
            pe.wait_ge(norm_split, SPLIT0[MLP_NORM])
            plain(S["uq_nope"], cq_hl, KQ)
            plain(S["uq_rope"], cq_hl, KQ)
            plain(S["ukv_k"], ckv_hl, KKV)
            plain(S["ukv_v"], ckv_hl, KKV, values=True)
            pe.wait_ge(rope_ready, 3)
            pe.wait_ge(group_out, S["ukv_v"].g0 + S["ukv_v"].groups)
            pe.wait_ge(o_split, HEADS // 2)
            attend(S["y_fox"], o_fox, HEADS, "mla")
            pe.wait_ge(o_split, HEADS)
            plain(S["y_mla"], o_mla, HEADS)

            def merged_ready(ui):
                pe.wait_ge(full_split, 2 * (ui + 1))
            plain(S["w_out"], m_hl, KT, ready=merged_ready)
            norm_sum(MLP_NORM, 4, [[sq[:, j % 2, 0], sq[:, j % 2, 1]] for j in range(KT // 2)])
            for i in range(MLP_PARTS):
                plain(S[f"up{i}"], hn_hl, KT, ready=norm_ready(MLP_NORM, SLABS))
                def hidden_ready(ui, base=FULL0[f"up{i}"]):
                    pe.wait_ge(full_split, base + 2 * (ui + 1))
                plain(S[f"down{i}"], u_hl, D_FF // P // MLP_PARTS, ready=hidden_ready)
            norm_sum(LAST_NORM, 4, [[sq[:, j % 2, 0], sq[:, j % 2, 1]] for j in range(KT // 2)])

        @block.scalar
        def _(act):
            def split_hi(stage, g, j):
                if stage.units == 0.5 and j % 2:
                    return
                for n, slot in slots_of(stage, g, j):
                    act.wait_ge(unit_loaded[slot], (n // RING + 1) * 16 if isinstance(n, int) else ring_turn(n, slot))
                    if not isinstance(n, int) or n >= RING:
                        units_free(n)
                    nc.scalar.activation(hl[:, slot, :, 0], raw[:, slot], ACT.Copy).then_inc(unit_hi, 1)

            def ring_turn(n, slot):
                return (n - slot) * (16 // RING) + 16

            def units_free(n):
                act.wait_ge(halves_used, n * 2 - 2 * (RING - 1))

            def low_half(stage, g, j):
                b0 = pair_of(stage, j)
                act.wait_ge(halves_used, halves_until(stage, g))
                if stage.g0 + j >= 2:
                    act.wait_ge(group_out, g + (stage.g0 - 1))
                scale = {"fq": FOX_SCALE, "uq_nope": MLA_SCALE, "uq_rope": MLA_SCALE}.get(stage.name, 1.0)
                n = 1 if stage.name == "krff" else 2
                nc.scalar.activation(part[:, (stage.g0 + j) % 2, 0:n], bank[:, b0:b0 + n, T:], ACT.Copy,
                                     scale=scale).then_inc(group_low, 1)

            def sum_squares(norm, kt, src):
                for j in range(kt // 2):
                    if j >= 2:
                        act.wait_ge(squares_used, SQ0[norm] + j - 1)
                    if norm == X_NORM and j % 2 == 0:
                        act.wait_ge(x_loaded[j // 2], 16)
                    nc.scalar.activation(sq[:, j % 2], src[:, 2 * j:2 * j + 2], ACT.Square).then_inc(squares, 1)

            def root(norm, b, d):
                pieces = 1 if norm in (Q_NORM, KV_NORM) else KT // 2
                act.wait_ge(squares_used, SQ0[norm] + pieces)
                nc.scalar.activation(std[:, norm % 2], bank[:, b, 0:T], ACT.Sqrt, scale=1.0 / d,
                                     bias=cst[:, C_EPS:C_EPS + 1]).then_inc(std_done, 1)

            def norm_his(norm, kt, src, dst, gcol):
                for k in range(kt):
                    if k % 2 == 0:
                        act.wait_ge(normed, NORMED0[norm] + k // 2 + 1)
                    nc.scalar.activation(dst[:, k, 0], src[:, k], ACT.Copy,
                                         scale=gain[:, gcol + k:gcol + k + 1]).then_inc(norm_hi, 1)

            def sigmoids(g):
                nc.scalar.activation(gate[:, bass.ds(2 * g, 2)], gate[:, bass.ds(2 * g, 2)],
                                     ACT.Sigmoid).then_inc(gate_done, 1)

            def exps(i):
                act.wait_ge(max_ready, i + 1)
                for hh in range(2):
                    for q, piece in ((0, slice(0, 1)), (1, slice(1, 3))):
                        c = 2 * q + hh
                        nc.scalar.activation(prob[:, hh, piece], prob[:, hh, piece], ACT.Exp,
                                             bias=cols[:, 1, c:c + 1],
                                             accum_out=cols[:, 2, c:c + 1]).then_inc(exp_done, 1)

            def prob_t_copy(i):
                act.wait_ge(transposed, i + 1)
                nc.scalar.activation(prob_t[:], bank[:, 6:8, 0:3 * P].rearrange("p b (k q) -> p b k q", k=3),
                                     ACT.Copy).then_inc(prob_t_ready, 1)

            def out_hi(i):
                dst = o_fox if i < 4 else o_mla
                act.wait_ge(mixed, i + 1)
                h = 2 * (i % 4)
                nc.scalar.activation(dst[:, h:h + 2, 0], bank[:, 6].rearrange("p (h t) -> p h t", h=2),
                                     ACT.Copy).then_inc(o_hi, 1)

            def attention_step(step, pair0):
                if step == -1:
                    exps(pair0)
                elif step % 2 == 0:
                    prob_t_copy(pair0 + step // 2)
                    if step < 6:
                        exps(pair0 + step // 2 + 1)
                else:
                    out_hi(pair0 + step // 2)

            def value_hi(stage, g, dst):
                f = g + FULL0[stage.name]
                act.wait_ge(full_ready, f + 1)
                nc.scalar.activation(dst[:, bass.ds(2 * g, 2), 0], full[:], ACT.Copy).then_inc(full_hi, 1)

            act.dma_start(cst[:], consts).then_inc(consts_in, 16)
            act.dma_start(gain[:], gains).then_inc(consts_in, 16)
            for i in range(4):
                act.dma_start(x_in[:, 4 * i:4 * i + 4], x_t[:, 4 * i:4 * i + 4]).then_inc(x_loaded[i], 16)

            prev = [None]

            def slots(stage, first=0, last=None, after=None):
                last = stage.groups if last is None else last
                if first == 0:
                    split_hi(stage, 0, 0)
                    if prev[0] is not None:
                        p_stage, p_after = prev[0]
                        low_half(p_stage, p_stage.groups - 1, p_stage.groups - 1)
                        if p_after is not None:
                            p_after(p_stage.groups - 1)
                    first = 1
                def body(g, j):
                    split_hi(stage, g, j)
                    low_half(stage, g - 1, j - 1)
                    if after is not None:
                        after(g - 1)
                run(act, stage, first, last, body)
                prev[0] = (stage, after)

            act.wait_ge(consts_in, 32)
            sum_squares(X_NORM, KT, x_in)
            split_hi(S["cq"], 0, 0)
            root(X_NORM, 4, D)
            norm_his(X_NORM, KT, xn, x_hl, G_ATTN)
            prev[0] = (S["cq"], None)
            slots(S["cq"], first=1)
            slots(S["ckv"])
            slots(S["krff"])
            slots(S["fq"], last=1)
            act.wait_ge(group_out, S["krff"].g0)
            nc.scalar.activation(cq_sq[:], cq_z[:], ACT.Square).then_inc(squares, 1)
            nc.scalar.activation(ckv_sq[:], ckv_z[:], ACT.Square).then_inc(squares, 1)
            slots(S["fq"], first=1, last=2)
            root(Q_NORM, 4, Q_LORA)
            root(KV_NORM, 5, KV_LORA)
            slots(S["fq"], first=2, last=3)
            norm_his(Q_NORM, KQ, cq_n, cq_hl, G_Q)
            norm_his(KV_NORM, KKV, ckv_n, ckv_hl, G_KV)
            slots(S["fq"], first=3)
            act.wait_ge(ff_abs, 1)
            nc.scalar.activation(ff_c[FF_A:], ff_b[FF_A:], ACT.Exp, scale=-1.0).then_inc(ff_exp, 1)
            act.wait_ge(ff_exp, 1)
            nc.scalar.activation(ff_b[FF_A:], ff_c[FF_A:], ACT.Ln,
                                 bias=cst[FF_A:, C_ONES:C_ONES + 1]).then_inc(ff_ln, 1)
            slots(S["fk"])
            slots(S["fv"])
            for g in range(8):
                if g == 0:
                    slots(S["gates"], last=1)
                else:
                    slots(S["gates"], first=g, last=g + 1)
                attention_step(g - 1, 0)
            slots(S["gates"], first=8, last=9)
            attention_step(7, 0)

            def two_sigmoids(g, j):
                split_hi(S["gates"], g, j)
                low_half(S["gates"], g - 1, j - 1)
                act.wait_ge(group_out, g + (S["gates"].g0 - 1))
                sigmoids(g - 2)
                sigmoids(g - 9)
            run(act, S["gates"], 9, 16, two_sigmoids)
            slots(S["uq_nope"], last=1)
            act.wait_ge(group_out, S["gates"].g0 + S["gates"].groups - 1)
            sigmoids(S["gates"].groups - 2)
            slots(S["uq_nope"], first=1, last=2)
            act.wait_ge(group_out, S["gates"].g0 + S["gates"].groups)
            sigmoids(S["gates"].groups - 1)
            slots(S["uq_nope"], first=2)
            slots(S["uq_rope"])
            slots(S["ukv_k"])
            slots(S["ukv_v"])
            for g in range(8):
                slots(S["y_fox"], first=g, last=g + 1)
                attention_step(g - 1, 4)
            slots(S["y_mla"], last=1)
            attention_step(7, 4)
            merged = lambda g: value_hi(S["y_mla"], g, m_hl)
            slots(S["y_mla"], first=1, after=merged)
            slots(S["w_out"])

            def hidden(stage):
                return lambda g: value_hi(stage, g, u_hl)
            for i in range(MLP_PARTS):
                up, down = S[f"up{i}"], S[f"down{i}"]
                if i == 0:
                    slots(up, last=1)
                    act.wait_ge(resid_done, S["w_out"].groups)
                    sum_squares(MLP_NORM, KT, resid)
                    root(MLP_NORM, 4, D)
                    norm_his(MLP_NORM, KT, xn, hn_hl, G_MLP)
                    slots(up, first=1, after=hidden(up))
                else:
                    slots(up, after=hidden(up))
                slots(down)
            low_half(down, down.groups - 1, down.groups - 1)
            act.wait_ge(resid_done, 3 * S["w_out"].groups)
            sum_squares(LAST_NORM, KT, resid)
            root(LAST_NORM, 4, D)
            for k in range(KT):
                if k % 2 == 0:
                    act.wait_ge(normed, NORMED0[LAST_NORM] + k // 2 + 1)
                nc.scalar.activation(final[:, k], last_n[:, k], ACT.Copy,
                                     scale=gain[:, G_FINAL + k:G_FINAL + k + 1]).then_inc(final_done, 1)

        @block.vector
        def _(dve):
            steps = [0]

            def then_wait(ins):
                steps[0] += 1
                ins.then_inc(vec_step, 1)
                dve.wait_ge(vec_step, steps[0])

            def split_lo(stage, g, j):
                if stage.units == 0.5 and j % 2:
                    return
                for n, slot in slots_of(stage, g, j):
                    dve.wait_ge(unit_hi, n + 1)
                    nc.vector.tensor_tensor(hl[:, slot, :, 1], raw[:, slot], hl[:, slot, :, 0].bitcast(F32),
                                            ALU.subtract).then_inc(unit_split, 1)

            def high_half(stage, g, j):
                b0 = pair_of(stage, j)
                dve.wait_ge(group_low, g + (stage.g0 + 1))
                low, name = part[:, (stage.g0 + j) % 2], stage.name
                two = bass.ds(2 * g, 2)
                dst = {"cq": lambda: cq_z[:, two], "ckv": lambda: ckv_z[:, two],
                       "krff": lambda: kr_z[:], "fq": lambda: fq[:, two], "fk": lambda: fk[:, two],
                       "fv": lambda: v_fox[:, :, bass.ds(COLS * g, COLS)], "gates": lambda: gate[:, two],
                       "uq_nope": lambda: qn[:, two], "uq_rope": lambda: qr_z[:],
                       "ukv_k": lambda: kn[:, two],
                       "ukv_v": lambda: v_mla[:, :, bass.ds(COLS * g, COLS)]}.get(name, lambda: zsum[:])()
                high = bank[:, b0:b0 + 2, 0:T]
                if name == "krff":
                    high, low = bank[:, b0, 0:T], low[:, 0]
                if name in ("fq", "uq_nope", "uq_rope"):
                    scale = FOX_SCALE if name == "fq" else MLA_SCALE
                    ins = nc.vector.scalar_tensor_tensor(dst, high, scale, low, ALU.mult, ALU.add)
                else:
                    ins = nc.vector.tensor_tensor(dst, high, low, ALU.add)
                ins.then_inc(group_out, 1)

            def summed(stage, g):
                dve.wait_ge(group_out, g + (stage.g0 + 1))

            def norm(norm, kt, src, tmp, dst, gcol):
                dve.wait_ge(std_done, norm + 1)
                then_wait(nc.vector.reciprocal(rstd[:, norm % 2], std[:, norm % 2]))
                r = rstd[:, norm % 2].unsqueeze(1).broadcast_to([P, 2, T])
                for j in range(kt // 2):
                    nc.vector.tensor_tensor(tmp[:, 2 * j:2 * j + 2], src[:, 2 * j:2 * j + 2], r,
                                            ALU.mult).then_inc(normed, 1)
                if dst is None:
                    return
                for k in range(kt):
                    dve.wait_ge(norm_hi, SPLIT0[norm] + k + 1)
                    nc.vector.scalar_tensor_tensor(dst[:, k, 1], tmp[:, k], gain[:, gcol + k:gcol + k + 1],
                                                   dst[:, k, 0].bitcast(F32), ALU.mult,
                                                   ALU.subtract).then_inc(norm_split, 1)

            def rotary(z, swap, sin_part, dst, rows, extra):
                for q in range(0, rows, 32):
                    ins = nc.vector.tensor_copy(swap[q:q + 32], z[q ^ 32:(q ^ 32) + 32])
                then_wait(ins)
                shape = [rows, extra, T] if extra else [rows, T]
                table = lambda c: (cst[0:rows, c:c + T].unsqueeze(1).broadcast_to(shape) if extra
                                   else cst[0:rows, c:c + T])
                then_wait(nc.vector.tensor_tensor(sin_part, swap[0:rows], table(C_SIN), ALU.mult))
                then_wait(nc.vector.tensor_tensor(z[0:rows], z[0:rows], table(C_COS), ALU.mult))
                return nc.vector.tensor_tensor(dst, z[0:rows], sin_part, ALU.add)

            def forget_logits():
                f = slice(FF_A, P)
                then_wait(nc.vector.tensor_scalar(ff_a[f], kr_z[f], gain[f, G_FBIAS:G_FBIAS + 1], None, ALU.add))
                then_wait(nc.vector.scalar_tensor_tensor(ff_b[f], ff_a[f], -1.0, ff_a[f], ALU.mult, ALU.max))
                nc.vector.tensor_scalar(ff_a[f], ff_a[f], 0.0, None, ALU.min).then_inc(ff_abs, 1)
                dve.wait_ge(ff_abs, 1)

            def forget_sums():
                f = slice(FF_A, P)
                dve.wait_ge(ff_ln, 1)
                then_wait(nc.vector.tensor_tensor(ff_a[f], ff_a[f], ff_b[f], ALU.subtract))
                then_wait(nc.vector.tensor_tensor_scan(ff_c[f], cst[f, C_ONES:C_ONES + T], ff_a[f], 0.0,
                                                       ALU.mult, ALU.add))
                then_wait(nc.vector.tensor_scalar(left[f], ff_c[f], cst[f, C_LEFT:C_LEFT + 1],
                                                  cst[f, C_LEFT + 1:C_LEFT + 2], ALU.mult, ALU.add))

            def bias_factor(i):
                f = slice(FF_A, P)
                if i:
                    dve.wait_ge(scored, i)
                for hh in range(2):
                    h = 2 * i + hh
                    ins = nc.vector.tensor_scalar(right[f, hh], ff_c[f], cst[f, C_RIGHT_M + h:C_RIGHT_M + h + 1],
                                                  cst[f, C_RIGHT_N + h:C_RIGHT_N + h + 1], ALU.mult, ALU.add)
                ins.then_inc(bias_ready, 1)

            def maxima(i):
                dve.wait_ge(scored, i + 1)
                c = C_MASK_FOX if i < 4 else C_MASK_MLA
                mask = cst[:, c:c + 3 * P].unsqueeze(1).broadcast_to([P, 2, 3 * P])
                then_wait(nc.vector.tensor_tensor(prob[:].rearrange("p h k q -> p h (k q)"), bank[:, 4:6, 0:3 * P],
                                                  mask, ALU.add))
                nc.vector.tensor_reduce(cols[:, 0, 0:2], prob[:, :, 0], AX.X, ALU.max)
                then_wait(nc.vector.tensor_reduce(cols[:, 0, 2:4], prob[:, :, 1:3].rearrange("p h k q -> p h (k q)"),
                                                  AX.X, ALU.max))
                nc.vector.tensor_scalar(cols[:, 1], cols[:, 0], -1.0, None, ALU.mult).then_inc(max_ready, 1)
                if i < 3:
                    bias_factor(i + 1)

            def normalize(i):
                dve.wait_ge(exp_done, 4 * (i + 1))
                then_wait(nc.vector.reciprocal(cols[:, 3], cols[:, 2]))
                for hh in range(2):
                    for q, piece in ((0, slice(0, 1)), (1, slice(1, 3))):
                        c = 2 * q + hh
                        ins = nc.vector.tensor_scalar(prob[:, hh, piece], prob[:, hh, piece],
                                                      cols[:, 3, c:c + 1], None, ALU.mult)
                ins.then_inc(prob_ready, 1)

            def out_lo(i):
                dst = o_fox if i < 4 else o_mla
                dve.wait_ge(o_hi, i + 1)
                h = 2 * (i % 4)
                nc.vector.tensor_tensor(dst[:, h:h + 2, 1], bank[:, 6].rearrange("p (h t) -> p h t", h=2),
                                        dst[:, h:h + 2, 0].bitcast(F32), ALU.subtract).then_inc(o_split, 1)

            def attention_step(step, pair0):
                if step == -1:
                    maxima(pair0)
                    normalize(pair0)
                elif step % 2 == 0:
                    if step < 6:
                        maxima(pair0 + step // 2 + 1)
                        normalize(pair0 + step // 2 + 1)
                else:
                    out_lo(pair0 + step // 2)

            def value_lo(stage, g, dst):
                f = g + FULL0[stage.name]
                dve.wait_ge(full_hi, f + 1)
                nc.vector.tensor_tensor(dst[:, bass.ds(2 * g, 2), 1], full[:],
                                        dst[:, bass.ds(2 * g, 2), 0].bitcast(F32),
                                        ALU.subtract).then_inc(full_split, 1)

            prev = [None]

            def slots(stage, first=0, last=None, after=None):
                last = stage.groups if last is None else last
                if first == 0:
                    split_lo(stage, 0, 0)
                    if prev[0] is not None:
                        p_stage, p_after = prev[0]
                        high_half(p_stage, p_stage.groups - 1, p_stage.groups - 1)
                        if p_after is not None:
                            p_after(p_stage.groups - 1)
                    first = 1
                def body(g, j):
                    split_lo(stage, g, j)
                    high_half(stage, g - 1, j - 1)
                    if after is not None:
                        after(g - 1)
                run(dve, stage, first, last, body)
                prev[0] = (stage, after)

            split_lo(S["cq"], 0, 0)
            dve.wait_ge(consts_in, 32)
            for i in range(4):
                dve.wait_ge(x_loaded[i], 16)
            norm(X_NORM, KT, x_in, xn, x_hl, G_ATTN)
            prev[0] = (S["cq"], None)
            slots(S["cq"], first=1)
            slots(S["ckv"])
            slots(S["krff"])
            slots(S["fq"], last=1)
            summed(S["krff"], 0)
            dve.wait_ge(zeroed, 3)
            then_wait(rotary(kr_z, kr_swap, ff_b[0:ROPE], k_rope[0:ROPE, 0], ROPE, 0))
            nc.vector.tensor_copy(k_rope[ROPE:, 1], k_rope[0:ROPE, 0]).then_inc(rope_ready, 1)
            slots(S["fq"], first=1, last=2)
            forget_logits()
            slots(S["fq"], first=2, last=3)
            norm(Q_NORM, KQ, cq_z, cq_n, cq_hl, G_Q)
            norm(KV_NORM, KKV, ckv_z, ckv_n, ckv_hl, G_KV)
            slots(S["fq"], first=3)
            slots(S["fk"])
            forget_sums()
            bias_factor(0)
            slots(S["fv"])
            for g in range(8):
                slots(S["gates"], first=g, last=g + 1)
                attention_step(g - 1, 0)
            slots(S["gates"], first=8, last=9)
            attention_step(7, 0)
            slots(S["gates"], first=9)
            slots(S["uq_nope"])

            def turn_queries(g):
                summed(S["uq_rope"], g)
                rotary(qr_z, qr_swap, qr_sin[:], qr[:, 2 * g:2 * g + 2], P, 2).then_inc(rope_ready, 1)
                dve.wait_ge(rope_ready, g + 2)
            slots(S["uq_rope"], after=turn_queries)
            slots(S["ukv_k"])
            slots(S["ukv_v"])

            def fox_gated(g):
                summed(S["y_fox"], g)
                gs = slice(KT + 2 * g, KT + 2 * g + 2)
                then_wait(nc.vector.tensor_tensor(gate[:, gs], gate[:, gs], zsum[:], ALU.mult))
            dve.wait_ge(gate_done, S["gates"].groups)
            for g in range(8):
                slots(S["y_fox"], first=g, last=g + 1, after=fox_gated)
                attention_step(g - 1, 4)

            def merge(g):
                summed(S["y_mla"], g)
                nc.vector.tensor_tensor(zsum[:], zsum[:], gate[:, bass.ds(2 * g, 2)], ALU.mult).then_inc(weighted, 1)
                dve.wait_ge(weighted, g + 1)
                nc.vector.tensor_tensor(full[:], zsum[:], gate[:, bass.ds(2 * g + KT, 2)],
                                        ALU.add).then_inc(full_ready, 1)
                dve.wait_ge(full_ready, g + 1)
                value_lo(S["y_mla"], g, m_hl)
            slots(S["y_mla"], last=1)
            attention_step(7, 4)
            slots(S["y_mla"], first=1, after=merge)

            def add_resid(stage):
                def after(g):
                    summed(stage, g)
                    two = bass.ds(2 * g, 2)
                    nc.vector.tensor_tensor(resid[:, two], resid[:, two], zsum[:], ALU.add).then_inc(resid_done, 1)
                    k = {"w_out": 0, "down0": 1, "down1": 2}[stage.name]
                    dve.wait_ge(resid_done, g + (k * stage.groups + 1))
                return after
            dve.wait_ge(resid_in, 16)
            slots(S["w_out"], after=add_resid(S["w_out"]))

            def hidden(stage):
                def after(g):
                    summed(stage, g)
                    nc.vector.scalar_tensor_tensor(full[:], zsum[:], 0.0, zsum[:], ALU.max,
                                                   ALU.mult).then_inc(full_ready, 1)
                    dve.wait_ge(full_ready, g + (FULL0[stage.name] + 1))
                    value_lo(stage, g, u_hl)
                return after
            for i in range(MLP_PARTS):
                up, down = S[f"up{i}"], S[f"down{i}"]
                if i == 0:
                    slots(up, last=1)
                    norm(MLP_NORM, KT, resid, xn, hn_hl, G_MLP)
                    slots(up, first=1, after=hidden(up))
                else:
                    slots(up, after=hidden(up))
                slots(down, after=add_resid(down))
            high_half(down, down.groups - 1, down.groups - 1)
            add_resid(down)(down.groups - 1)
            norm(LAST_NORM, KT, resid, last_n, None, G_FINAL)


def pack_stream(w_in, w_uq, w_ukv, w_mla_branch, w_fox_branch, w_out, w_up, w_down):
    stream = np.empty((N_UNITS, P, SLABS, COLS), w_in.dtype)
    at = [0]

    def columns(w, k_first=0, k_count=None):
        k_count = w.shape[0] // P if k_count is None else k_count
        w = w[k_first * P:(k_first + k_count) * P]
        groups = w.shape[1] // COLS
        units = (k_count // SLABS) * groups
        v = w.reshape(k_count // SLABS, SLABS, P, groups, COLS)
        stream[at[0]:at[0] + units] = v.transpose(3, 0, 2, 1, 4).reshape(units, P, SLABS, COLS)
        at[0] += units

    def half_units(w):
        v = w.reshape(2, P, w.shape[1] // COLS // 2, 2, COLS)
        units = w.shape[1] // COLS // 2
        stream[at[0]:at[0] + units] = v.transpose(2, 1, 3, 0, 4).reshape(units, P, SLABS, COLS)
        at[0] += units

    columns(w_in[:, 0:OFF_CKV])
    columns(w_in[:, OFF_CKV:OFF_KR])
    forget = w_in[:, OFF_FF:OFF_FF + 32]
    narrow = np.concatenate([w_in[:, OFF_KR:OFF_FQ], forget, forget], axis=1)
    v = narrow.reshape(KT // SLABS // 2, SLABS, 2, P, P)
    stream[at[0]:at[0] + 2] = v.transpose(0, 3, 1, 2, 4).reshape(2, P, SLABS, COLS)
    at[0] += 2
    for first in (OFF_FQ, OFF_FK, OFF_FV):
        columns(w_in[:, first:first + HEADS * DH])
    columns(w_in[:, OFF_G:])
    uq = w_uq.reshape(Q_LORA, HEADS, DH + ROPE)
    columns(uq[:, :, :DH].reshape(Q_LORA, HEADS * DH))
    columns(uq[:, :, DH:].reshape(Q_LORA, HEADS * ROPE))
    ukv = w_ukv.reshape(KV_LORA, HEADS, 2, DH)
    half_units(ukv[:, :, 0].reshape(KV_LORA, HEADS * DH))
    half_units(ukv[:, :, 1].reshape(KV_LORA, HEADS * DH))
    columns(w_fox_branch)
    columns(w_mla_branch)
    columns(w_out)
    per = D_FF // MLP_PARTS
    for i in range(MLP_PARTS):
        columns(w_up[:, i * per:(i + 1) * per])
        columns(w_down, i * per // P, per // P)
    assert at[0] == N_UNITS
    return stream


def kernel(x, attn_norm, w_in, fox_f_bias, q_norm, w_uq, kv_norm, w_ukv,
           w_mla_branch, w_fox_branch, w_out, mlp_norm, w_up, w_down, final_norm):
    import concourse.bacc as bacc
    from concourse.bass_utils import run_bass_kernel_spmd

    a = np.asarray
    stream = pack_stream(a(w_in)[0], a(w_uq)[0], a(w_ukv)[0], a(w_mla_branch)[0], a(w_fox_branch)[0],
                         a(w_out)[0], a(w_up)[0], a(w_down)[0])
    x_t = np.ascontiguousarray(a(x)[0].T.reshape(KT, P, T).transpose(1, 0, 2))
    gains = np.zeros((P, G_COUNT), np.float32)
    for col, g in ((G_ATTN, a(attn_norm)[0]), (G_Q, a(q_norm)[0]), (G_KV, a(kv_norm)[0]),
                   (G_MLP, a(mlp_norm)[0]), (G_FINAL, a(final_norm))):
        gains[:, col:col + g.size // P] = g.reshape(-1, P).T
    for row in (FF_A, FF_B):
        gains[row:row + HEADS, G_FBIAS] = a(fox_f_bias)[0]

    nc = bacc.Bacc("TRN2", target_bir_lowering=False, num_devices=1)
    arrays = {"weights": stream, "x_t": x_t, "consts": constants(), "gains": gains}
    aps = [nc.dram_tensor(k, v.shape, F32, kind="ExternalInput").ap() for k, v in arrays.items()]
    out_t = nc.dram_tensor("out_t", (P, KT, T), F32, kind="ExternalOutput").ap()
    program(nc, *aps, out_t)
    r = run_bass_kernel_spmd(nc, [arrays], core_ids=[0])
    y = r.results[0]["out_t"]
    return np.ascontiguousarray(y.transpose(1, 0, 2).reshape(D, T).T)[None]
```

```python
import math
from contextlib import ExitStack

import numpy as np
import concourse.bass as bass
from concourse import mybir

F32 = mybir.dt.float32
F32R = mybir.dt.float32r
ALU = mybir.AluOpType
ACT = mybir.ActivationFunctionType
AX = mybir.AxisListType

P = 128
D = 2048
T = 256
TB = T // P
CHUNK = 64
HEADS = 8
DH = 128
ROPE = 64
Q_LORA, KV_LORA = 512, 256
D_FF = 4 * D
ROPE_THETA = 10000.0
EPS = 1e-6
KT = D // P
KQ, KKV = Q_LORA // P, KV_LORA // P

OFF_CKV = Q_LORA
OFF_KR = OFF_CKV + KV_LORA
OFF_FQ = OFF_KR + ROPE
OFF_FK = OFF_FQ + HEADS * DH
OFF_FV = OFF_FK + HEADS * DH
OFF_FF = OFF_FV + HEADS * DH
OFF_G = OFF_FF + HEADS

SLABS, COLS = 4, 256
UNIT = SLABS * COLS
RING = 4
MLP_PARTS = 2
FF_GROUPS = D_FF // COLS // MLP_PARTS

FOX_SCALE = 1.0 / math.sqrt(DH)
MLA_SCALE = 1.0 / math.sqrt(DH + ROPE)
MASKED = -3.0e38

FF_A, FF_B = 64, 96


class Stage:
    def __init__(self, name, groups, units):
        self.name, self.groups, self.units = name, groups, units
        self.g0 = self.u0 = 0


def make_stages():
    stages = [
        Stage("cq", Q_LORA // COLS, KT // SLABS),
        Stage("ckv", KV_LORA // COLS, KT // SLABS),
        Stage("krff", 1, KT // SLABS // 2),
        Stage("fq", HEADS * DH // COLS, KT // SLABS),
        Stage("fk", HEADS * DH // COLS, KT // SLABS),
        Stage("fv", HEADS * DH // COLS, KT // SLABS),
        Stage("gates", 2 * D // COLS, KT // SLABS),
        Stage("uq_nope", HEADS * DH // COLS, KQ // SLABS),
        Stage("uq_rope", HEADS * ROPE // COLS, KQ // SLABS),
        Stage("ukv_k", HEADS * DH // COLS, 0.5),
        Stage("ukv_v", HEADS * DH // COLS, 0.5),
        Stage("y_fox", D // COLS, HEADS // SLABS),
        Stage("y_mla", D // COLS, HEADS // SLABS),
        Stage("w_out", D // COLS, KT // SLABS),
    ]
    for part in range(MLP_PARTS):
        stages.append(Stage(f"up{part}", FF_GROUPS, KT // SLABS))
        stages.append(Stage(f"down{part}", D // COLS, D_FF // P // MLP_PARTS // SLABS))
    g = u = 0
    for s in stages:
        s.g0, s.u0 = g, u
        g += s.groups
        u += int(s.groups * s.units)
    return stages, g, u


STAGES, N_GROUPS, N_UNITS = make_stages()
S = {s.name: s for s in STAGES}
assert N_UNITS % RING == 0

C_IDENT = 0
C_MASK_FOX = C_IDENT + P
C_MASK_MLA = C_MASK_FOX + 3 * P
C_COS = C_MASK_MLA + 3 * P
C_SIN = C_COS + T
C_ONES = C_SIN + T
C_LEFT = C_ONES + T
C_RIGHT_M = C_LEFT + 2
C_RIGHT_N = C_RIGHT_M + HEADS
C_EPS = C_RIGHT_N + HEADS
C_COUNT = C_EPS + 1

G_ATTN = 0
G_Q = G_ATTN + KT
G_KV = G_Q + KQ
G_MLP = G_KV + KKV
G_FINAL = G_MLP + KT
G_FBIAS = G_FINAL + KT
G_COUNT = G_FBIAS + 1


def constants():
    c = np.zeros((P, C_COUNT), np.float32)
    p = np.arange(P)
    c[:, C_IDENT:C_IDENT + P] = np.eye(P)
    for col, keep in ((C_MASK_FOX, p[None, :] <= p[:, None]),
                      (C_MASK_MLA, p[None, :] // CHUNK <= p[:, None] // CHUNK)):
        diagonal = np.where(keep, 0.0, MASKED)
        c[:, col:col + P] = diagonal
        c[:, col + 2 * P:col + 3 * P] = diagonal
    half = ROPE // 2
    inv = np.float32(1.0) / np.power(np.float32(ROPE_THETA),
                                     np.arange(0, ROPE, 2, dtype=np.float32) / np.float32(ROPE))
    angle = (inv[p % half][:, None] * np.arange(T, dtype=np.float32)[None, :]).astype(np.float32)
    c[:, C_COS:C_COS + T] = np.cos(angle)
    c[:, C_SIN:C_SIN + T] = np.where(p % ROPE < half, -1.0, 1.0)[:, None] * np.sin(angle)
    c[:, C_ONES:C_ONES + T] = 1.0
    c[FF_B:FF_B + HEADS, C_LEFT] = 1.0
    c[FF_A:FF_A + HEADS, C_LEFT + 1] = 1.0
    for h in range(HEADS):
        c[FF_A + h, C_RIGHT_M + h] = -1.0
        c[FF_B + h, C_RIGHT_N + h] = 1.0
    c[:, C_EPS] = EPS
    return c


def program(nc, stream, x_t, consts, gains, out_t):
    sbuf0 = (nc.sbuf_base + 511) // 512 * 512
    kib = 1024

    def at(name, offset, *shape, dt=F32):
        return nc.alloc_sbuf_tensor_at(name, [P, *shape], dt, offset=sbuf0 + offset)

    raw = at("raw", 0, RING, SLABS, COLS)
    hl = at("hl", 16 * kib, RING, SLABS, 2, COLS, dt=F32R)
    H = 48 * kib
    o_fox = at("o_fox", H, HEADS, 2, T, dt=F32R)
    resid = at("resid", H, KT, T)
    o = H + 16 * kib
    cst = at("cst", o, C_COUNT)
    gain = at("gain", o + 8 * kib, G_COUNT)
    cols = at("cols", o + 8 * kib + 512, 4, 4)
    part = at("part", o + 9 * kib, 2, 2, T)
    zsum = at("zsum", o + 13 * kib, 2, T)
    std = at("std", o + 15 * kib, 2, T)
    prob = at("prob", o + 19 * kib, 2, 3, P)
    prob_t = at("prob_t", o + 22 * kib, 2, 3, P)
    full = at("full", o + 19 * kib, 2, T)
    relu = at("relu", o + 17 * kib, 2, T)
    assert C_COUNT * 4 <= 8 * kib and G_COUNT * 4 <= 512
    A = o + 25 * kib
    x_hl = at("x_hl", A, KT, 2, T, dt=F32R)
    qn = at("qn", A, HEADS, T)
    kn = at("kn", A + 8 * kib, HEADS, T)
    v_mla = at("v_mla", A + 16 * kib, TB, HEADS * DH)
    qr = at("qr", A + 24 * kib, HEADS // 2, T)
    m_hl = at("m_hl", A, KT, 2, T, dt=F32R)
    B = A + 32 * kib
    fq = at("fq", B, HEADS, T)
    fk = at("fk", B + 8 * kib, HEADS, T)
    v_fox = at("v_fox", B + 16 * kib, TB, HEADS * DH)
    cq_hl = at("cq_hl", B + 24 * kib, KQ, 2, T, dt=F32R)
    o_mla = at("o_mla", B, HEADS, 2, T, dt=F32R)
    qr_z = at("qr_z", B + 16 * kib, 2, T)
    qr_swap = at("qr_swap", B + 18 * kib, 2, T)
    qr_sin = at("qr_sin", B + 20 * kib, 2, T)
    x_sq = at("x_sq", B, 4, 4, T)
    x_gain = at("x_gain", B + 16 * kib, KT, T)
    u_hl = at("u_hl", A, D_FF // P // MLP_PARTS, 2, T, dt=F32R)
    C = B + 32 * kib
    x_in = at("x_in", C, KT, T)
    gate = at("gate", C, 2 * KT, T)
    cq_z = at("cq_z", C, KQ, T)
    ckv_z = at("ckv_z", C + 4 * kib, KKV, T)
    cq_sq = at("cq_sq", C + 6 * kib, KQ, T)
    ckv_sq = at("ckv_sq", C + 10 * kib, KKV, T)
    cq_n = at("cq_n", C + 12 * kib, KQ, T)
    ckv_n = at("ckv_n", C + 16 * kib, KKV, T)
    kr_z = at("kr_z", C + 18 * kib, T)
    kr_swap = at("kr_swap", C + 19 * kib, T)
    ff_a = at("ff_a", C + 20 * kib, T)
    ff_b = at("ff_b", C + 21 * kib, T)
    ff_c = at("ff_c", C + 22 * kib, T)
    final_gain = at("final_gain", C, KT, T)
    final = at("final", C + 16 * kib, KT, T)
    hn_hl = at("hn_hl", C, KT, 2, T, dt=F32R)
    E = C + 32 * kib
    ckv_hl = at("ckv_hl", E, KKV, 2, T, dt=F32R)
    k_rope = at("k_rope", E + 4 * kib, 2, T)
    left = at("left", E + 6 * kib, T)
    right = at("right", E + 7 * kib, 2, T)
    rstd = at("rstd", E + 9 * kib, 5, T)
    rstd_col = at("rstd_col", E + 14 * kib, TB)
    sq = at("sq", E + 15 * kib, 2, T)
    sq_sum = at("sq_sum", E + 17 * kib, 2, 2, T)
    assert sbuf0 + E + 21 * kib <= nc.sbuf_usable_end, (sbuf0 + E + 21 * kib, nc.sbuf_usable_end)

    ctx = ExitStack()
    with ctx:
        sem = lambda name: ctx.enter_context(nc.semaphore(name))
        bank = ctx.enter_context(nc.psum_tensor("bank", [P, 8, 512], F32))

        unit_loaded = [sem(f"unit_loaded{i}") for i in range(RING)]
        unit_hi = sem("unit_hi")
        unit_split = sem("unit_split")
        halves_used = sem("halves_used")
        group_low = sem("group_low")
        group_out = sem("group_out")
        consts_in = sem("consts_in")
        x_loaded = [sem(f"x_loaded{i}") for i in range(4)]
        resid_in = sem("resid_in")
        zeroed = sem("zeroed")
        x_gained = sem("x_gained")
        x_hi = sem("x_hi")
        x_split = sem("x_split")
        x_squared = sem("x_squared")
        tree = sem("tree")
        squares_ready = sem("squares_ready")
        squares_summed = sem("squares_summed")
        std_done = sem("std_done")
        rstd_ready = sem("rstd_ready")
        rstd_turned = sem("rstd_turned")
        scaled = sem("scaled")
        normed = sem("normed")
        norm_hi = sem("norm_hi")
        norm_split = sem("norm_split")
        rope_ready = sem("rope_ready")
        weighted = sem("weighted")
        ff_exp = sem("ff_exp")
        ff_ln = sem("ff_ln")
        ff_abs = sem("ff_abs")
        bias_ready = sem("bias_ready")
        scored = sem("scored")
        max_ready = sem("max_ready")
        exp_done = sem("exp_done")
        prob_ready = sem("prob_ready")
        transposed = sem("transposed")
        prob_t_ready = sem("prob_t_ready")
        mixed = sem("mixed")
        o_hi = sem("o_hi")
        o_split = sem("o_split")
        gate_done = sem("gate_done")
        full_ready = sem("full_ready")
        full_hi = sem("full_hi")
        full_split = sem("full_split")
        relu_ready = sem("relu_ready")
        resid_done = sem("resid_done")
        resid_squared = sem("resid_squared")
        resid_summed = sem("resid_summed")
        resid_hi = sem("resid_hi")
        resid_split = sem("resid_split")
        gain_done = sem("gain_done")
        final_done = sem("final_done")
        stored = sem("stored")
        vec_step = sem("vec_step")

        block = ctx.enter_context(nc.Block())

        FULL0 = {"y_mla": 0}
        for i in range(MLP_PARTS):
            FULL0[f"up{i}"] = S["y_mla"].groups + i * FF_GROUPS
        X_NORM, Q_NORM, KV_NORM, MLP_NORM, LAST_NORM = range(5)
        NORMED0 = {Q_NORM: 0, KV_NORM: KQ // 2}
        SPLIT0 = {Q_NORM: 0, KV_NORM: KQ}
        RESID0 = {"w_out": 0, "down0": S["w_out"].groups, "down1": 2 * S["w_out"].groups}
        FROM_X = ("cq", "ckv", "krff", "fq", "fk", "fv", "gates")

        def run(eng, stage, first, last, body):
            if 2 * stage.units % RING:
                for g in range(first, last):
                    body(g, g)
                return
            if (last - first) % 2:
                body(first, first)
                first += 1
            if last - first == 2:
                body(first, first)
                body(first + 1, first + 1)
            elif last > first:
                with eng.Fori(0, (last - first) // 2) as i:
                    body(i * 2 + first, first)
                    body(i * 2 + (first + 1), first + 1)

        def slots_of(stage, g, j):
            if stage.units == 0.5:
                return [(stage.u0 + g // 2, (stage.u0 + j // 2) % RING)]
            n = stage.units
            return [(g * n + (stage.u0 + k), (stage.u0 + j * n + k) % RING) for k in range(n)]

        def pair_of(stage, j):
            return 2 * ((stage.g0 + j) % 2)

        def halves_until(stage, g):
            halves = int(2 * stage.units)
            return g * halves + (int(2 * stage.u0) + halves)

        @block.sync
        def _(sp):
            for n in range(RING):
                sp.dma_start(raw[:, n], stream[n]).then_inc(unit_loaded[n], 16)
            with sp.Fori(1, N_UNITS // RING) as turn:
                for k in range(RING):
                    sp.wait_ge(unit_split, turn * RING + (k + 1 - RING))
                    sp.dma_start(raw[:, k], stream[bass.ds(turn * RING + k, 1)].rearrange("a p s c -> p (a s) c"))\
                      .then_inc(unit_loaded[k], 16)
            for i in range(KT // 2):
                sp.wait_ge(final_done, i + 1)
                sp.dma_start(out_t[:, 2 * i:2 * i + 2], final[:, 2 * i:2 * i + 2]).then_inc(stored, 16)
            sp.wait_ge(stored, 16 * (KT // 2))

        @block.gpsimd
        def _(pool):
            pool.wait_ge(consts_in, 32)
            for i in range(4):
                q = slice(4 * i, 4 * i + 4)
                pool.wait_ge(x_loaded[i], 16)
                g4 = gain[:, G_ATTN + 4 * i:G_ATTN + 4 * i + 4].unsqueeze(2).broadcast_to([P, 4, T])
                nc.gpsimd.tensor_tensor(x_gain[:, q], x_in[:, q], g4, ALU.mult).then_inc(x_gained, 1)
            nc.gpsimd.memset(sq_sum[:], 0.0).then_inc(zeroed, 1)
            nc.gpsimd.memset(k_rope[:], 0.0).then_inc(zeroed, 1)
            nc.gpsimd.memset(left[:], 0.0).then_inc(zeroed, 1)
            nc.gpsimd.memset(right[:], 0.0).then_inc(zeroed, 1)
            pool.wait_ge(halves_used, halves_until(S["y_fox"], S["y_fox"].groups - 1))
            pool.dma_start(resid[:], x_t).then_inc(resid_in, 16)

        @block.tensor
        def _(pe):
            def norm_sum(norm, b, tiles):
                if norm in (MLP_NORM, LAST_NORM):
                    pe.wait_ge(resid_summed, (norm - MLP_NORM + 1) * S["w_out"].groups)
                else:
                    pe.wait_ge(squares_ready, norm + 1)
                for i, tile in enumerate(tiles):
                    last = nc.tensor.matmul(bank[:, b, 0:T], cst[:, C_ONES:C_ONES + P], tile,
                                            start=i == 0, stop=i == len(tiles) - 1)
                last.then_inc(squares_summed, 1)

            def group(stage, g, j, moving, k_tiles, values=False, narrow=False, ready=None):
                b0 = pair_of(stage, j)
                if stage.g0 + j >= 2:
                    pe.wait_ge(group_out, g + (stage.g0 - 1))
                k = 0
                units = slots_of(stage, g, j)
                for ui, (n, slot) in enumerate(units):
                    pe.wait_ge(unit_split, n + 1)
                    slabs = range(SLABS)
                    if stage.units == 0.5:
                        slabs = range(2 * (j % 2), 2 * (j % 2) + 2)
                    if ready is not None:
                        ready(ui)
                    for s in slabs:
                        for sub in range(2 if narrow else 1):
                            x = moving(k)
                            first, end = k == 0, k == k_tiles - 1
                            for b in range(1 if narrow else 2):
                                ps = bank[:, b0 + b]
                                at_ = P * (sub if narrow else b)
                                if values:
                                    tok = slice(b * P, b * P + P)
                                    nc.tensor.matmul(ps, x[:, 0, tok], hl[:, slot, s].rearrange("p h c -> p (h c)"),
                                                     start=first, stop=False)
                                    last = nc.tensor.matmul(ps[:, T:], x[:, 1, tok], hl[:, slot, s, 0],
                                                            start=False, stop=end)
                                else:
                                    nc.tensor.matmul(ps, hl[:, slot, s, 0, at_:at_ + P],
                                                     x.rearrange("p h t -> p (h t)"), start=first, stop=False)
                                    last = nc.tensor.matmul(ps[:, T:], hl[:, slot, s, 1, at_:at_ + P], x[:, 0],
                                                            start=False, stop=end)
                            k += 1
                        if s % 2:
                            last.then_inc(halves_used, 1)
                assert k == k_tiles

            def x_ready(ui):
                pe.wait_ge(x_split, ui + 1)

            def x_ready_then_sum(ui):
                if ui == 2:
                    norm_sum(X_NORM, 4, [x_sq[:, 0, k] for k in range(4)])

            def resid_ready(ui):
                pe.wait_ge(resid_split, 2 * (ui + 1))
                if ui == 3:
                    norm_sum(MLP_NORM, 4, [sq_sum[:, 0, k] for k in range(2)])

            def plain(stage, tile, k_tiles, first=0, last=None, **kw):
                last = stage.groups if last is None else last
                def body(g, j):
                    group(stage, g, j, lambda k: tile[:, k], k_tiles, **kw)
                run(pe, stage, first, last, body)

            def scores(i, branch):
                done = i + 4 * (branch == "mla")
                if done:
                    pe.wait_ge(max_ready, done)
                if branch == "fox":
                    pe.wait_ge(bias_ready, i + 1)
                for hh in range(2):
                    h = 2 * i + hh
                    for qs, ks, c0 in ((slice(0, P), slice(0, P), 0), (slice(P, T), slice(0, T), P)):
                        dst = bank[:, 4 + hh, c0:c0 + ks.stop]
                        if branch == "fox":
                            nc.tensor.matmul(dst, fq[:, h, qs], fk[:, h, ks], start=True, stop=False)
                            last = nc.tensor.matmul(dst, left[:, qs], right[:, hh, ks], start=False, stop=True)
                        else:
                            nc.tensor.matmul(dst, qn[:, h, qs], kn[:, h, ks], start=True, stop=False)
                            last = nc.tensor.matmul(dst, qr[:, i, qs], k_rope[:, hh, ks], start=False, stop=True)
                last.then_inc(scored, 1)

            def transposes(i, branch):
                done = i + 4 * (branch == "mla")
                pe.wait_ge(prob_ready, done + 1)
                if done:
                    pe.wait_ge(o_split, done)
                for hh in range(2):
                    for piece in range(3):
                        last = nc.tensor.transpose(bank[:, 6 + hh, piece * P:piece * P + P],
                                                   prob[:, hh, piece], cst[:, C_IDENT:C_IDENT + P])
                last.then_inc(transposed, 1)

            def mix(i, branch):
                v = v_fox if branch == "fox" else v_mla
                pe.wait_ge(prob_t_ready, i + 4 * (branch == "mla") + 1)
                for hh in range(2):
                    cs = slice((2 * i + hh) * DH, (2 * i + hh + 1) * DH)
                    nc.tensor.matmul(bank[:, 6, hh * T:hh * T + T], v[:, 0, cs],
                                     prob_t[:, hh, 0:2].rearrange("p b q -> p (b q)"), start=True, stop=False)
                    last = nc.tensor.matmul(bank[:, 6, hh * T + P:hh * T + T], v[:, 1, cs],
                                            prob_t[:, hh, 2], start=False, stop=True)
                last.then_inc(mixed, 1)

            def attend(stage, tile, k_tiles, branch, **kw):
                scores(0, branch)
                for g in range(8):
                    group(stage, g, g, lambda k: tile[:, k], k_tiles, **kw)
                    if g % 2 == 0:
                        transposes(g // 2, branch)
                        if g < 6:
                            scores(g // 2 + 1, branch)
                    else:
                        mix(g // 2, branch)

            pe.wait_ge(consts_in, 32)
            plain(S["cq"], x_hl, KT, last=1, ready=x_ready)
            plain(S["cq"], x_hl, KT, first=1, ready=x_ready_then_sum)
            plain(S["ckv"], x_hl, KT)
            plain(S["krff"], x_hl, KT, narrow=True)
            plain(S["fq"], x_hl, KT, last=1)
            pe.wait_ge(rstd_ready, X_NORM + 1)
            for tb in range(TB):
                last = nc.tensor.transpose(bank[:, 7, tb * P:tb * P + P], rstd[:, X_NORM, tb * P:tb * P + P],
                                           cst[:, C_IDENT:C_IDENT + P])
            last.then_inc(rstd_turned, 1)
            norm_sum(Q_NORM, 4, [cq_sq[:, k] for k in range(KQ)])
            norm_sum(KV_NORM, 5, [ckv_sq[:, k] for k in range(KKV)])
            plain(S["fq"], x_hl, KT, first=1)
            plain(S["fk"], x_hl, KT)
            plain(S["fv"], x_hl, KT, values=True)
            pe.wait_ge(scaled, S["fv"].g0 + S["fv"].groups)
            attend(S["gates"], x_hl, KT, "fox")
            plain(S["gates"], x_hl, KT, first=8)
            pe.wait_ge(norm_split, KQ + KKV)
            plain(S["uq_nope"], cq_hl, KQ)
            plain(S["uq_rope"], cq_hl, KQ)
            plain(S["ukv_k"], ckv_hl, KKV)
            plain(S["ukv_v"], ckv_hl, KKV, values=True)
            pe.wait_ge(rope_ready, 3)
            pe.wait_ge(group_out, S["ukv_v"].g0 + S["ukv_v"].groups)
            pe.wait_ge(o_split, HEADS // 2)
            attend(S["y_fox"], o_fox, HEADS, "mla")
            pe.wait_ge(o_split, HEADS)
            plain(S["y_mla"], o_mla, HEADS)

            def merged_ready(ui):
                pe.wait_ge(full_split, 2 * (ui + 1))
            plain(S["w_out"], m_hl, KT, ready=merged_ready)
            for i in range(MLP_PARTS):
                up = S[f"up{i}"]
                if i == 0:
                    plain(up, hn_hl, KT, last=1, ready=resid_ready)
                    plain(up, hn_hl, KT, first=1)
                else:
                    plain(up, hn_hl, KT)
                def hidden_ready(ui, base=FULL0[f"up{i}"]):
                    pe.wait_ge(full_split, base + 2 * (ui + 1))
                plain(S[f"down{i}"], u_hl, D_FF // P // MLP_PARTS, ready=hidden_ready)
            norm_sum(LAST_NORM, 4, [sq_sum[:, 1, k] for k in range(2)])

        @block.scalar
        def _(act):
            def split_hi(stage, g, j):
                if stage.units == 0.5 and j % 2:
                    return
                for n, slot in slots_of(stage, g, j):
                    unit_to_hi(n, slot)

            def unit_to_hi(n, slot):
                act.wait_ge(unit_loaded[slot], (n - slot) * (16 // RING) + 16)
                if not isinstance(n, int) or n >= RING:
                    units_free(n)
                nc.scalar.activation(hl[:, slot, :, 0], raw[:, slot], ACT.Copy).then_inc(unit_hi, 1)

            def units_free(n):
                act.wait_ge(halves_used, n * 2 - 2 * (RING - 1))

            def low_half(stage, g, j):
                b0 = pair_of(stage, j)
                act.wait_ge(halves_used, halves_until(stage, g))
                if stage.g0 + j >= 2:
                    act.wait_ge(group_out, g + (stage.g0 - 1))
                scale = {"fq": FOX_SCALE, "uq_nope": MLA_SCALE, "uq_rope": MLA_SCALE}.get(stage.name, 1.0)
                n = 1 if stage.name == "krff" else 2
                nc.scalar.activation(part[:, (stage.g0 + j) % 2, 0:n], bank[:, b0:b0 + n, T:], ACT.Copy,
                                     scale=scale).then_inc(group_low, 1)

            def root(norm, b, d):
                act.wait_ge(squares_summed, norm + 1)
                nc.scalar.activation(std[:, norm % 2], bank[:, b, 0:T], ACT.Sqrt, scale=1.0 / d,
                                     bias=cst[:, C_EPS:C_EPS + 1]).then_inc(std_done, 1)

            def square_resid(stage, g):
                act.wait_ge(resid_done, g + (RESID0[stage.name] + 1))
                nc.scalar.activation(sq[:], resid[:, bass.ds(2 * g, 2)], ACT.Square).then_inc(resid_squared, 1)

            def resid_gain(stage, g, j, dst, gcol, done):
                for b in range(2):
                    nc.scalar.activation(dst(bass.ds(2 * g + b, 1)), resid[:, bass.ds(2 * g + b, 1)], ACT.Copy,
                                         scale=gain[:, bass.ds(2 * g + (gcol + b), 1)]).then_inc(done, 1)

            def norm_his(norm, kt, src, dst, gcol):
                for k in range(kt):
                    if k % 2 == 0:
                        act.wait_ge(normed, NORMED0[norm] + k // 2 + 1)
                    nc.scalar.activation(dst[:, k, 0], src[:, k], ACT.Copy,
                                         scale=gain[:, gcol + k:gcol + k + 1]).then_inc(norm_hi, 1)

            def sigmoids(g):
                nc.scalar.activation(gate[:, bass.ds(2 * g, 2)], gate[:, bass.ds(2 * g, 2)],
                                     ACT.Sigmoid).then_inc(gate_done, 1)

            def exps(i):
                act.wait_ge(max_ready, i + 1)
                for hh in range(2):
                    for q, piece in ((0, slice(0, 1)), (1, slice(1, 3))):
                        c = 2 * q + hh
                        nc.scalar.activation(prob[:, hh, piece], prob[:, hh, piece], ACT.Exp,
                                             bias=cols[:, 1, c:c + 1],
                                             accum_out=cols[:, 2, c:c + 1]).then_inc(exp_done, 1)

            def prob_t_copy(i):
                act.wait_ge(transposed, i + 1)
                nc.scalar.activation(prob_t[:], bank[:, 6:8, 0:3 * P].rearrange("p b (k q) -> p b k q", k=3),
                                     ACT.Copy).then_inc(prob_t_ready, 1)

            def out_hi(i):
                dst = o_fox if i < 4 else o_mla
                act.wait_ge(mixed, i + 1)
                h = 2 * (i % 4)
                nc.scalar.activation(dst[:, h:h + 2, 0], bank[:, 6].rearrange("p (h t) -> p h t", h=2),
                                     ACT.Copy).then_inc(o_hi, 1)

            def attention_step(step, pair0):
                if step == -1:
                    exps(pair0)
                elif step % 2 == 0:
                    prob_t_copy(pair0 + step // 2)
                    if step < 6:
                        exps(pair0 + step // 2 + 1)
                else:
                    out_hi(pair0 + step // 2)

            def value_hi(stage, g, dst):
                f = g + FULL0[stage.name]
                if stage.name != "y_mla":
                    act.wait_ge(relu_ready, f + (1 - FULL0["up0"]))
                    nc.scalar.activation(full[:], relu[:], ACT.Square).then_inc(full_ready, 1)
                act.wait_ge(full_ready, f + 1)
                nc.scalar.activation(dst[:, bass.ds(2 * g, 2), 0], full[:], ACT.Copy).then_inc(full_hi, 1)

            act.dma_start(cst[:], consts).then_inc(consts_in, 16)
            act.dma_start(gain[:], gains).then_inc(consts_in, 16)
            for i in range(4):
                act.dma_start(x_in[:, 4 * i:4 * i + 4], x_t[:, 4 * i:4 * i + 4]).then_inc(x_loaded[i], 16)

            prev = [None]

            def slots(stage, first=0, last=None, after=None):
                last = stage.groups if last is None else last
                if first == 0:
                    split_hi(stage, 0, 0)
                    if prev[0] is not None:
                        p_stage, p_after = prev[0]
                        low_half(p_stage, p_stage.groups - 1, p_stage.groups - 1)
                        if p_after is not None:
                            p_after(p_stage.groups - 1, p_stage.groups - 1)
                    first = 1
                def body(g, j):
                    split_hi(stage, g, j)
                    low_half(stage, g - 1, j - 1)
                    if after is not None:
                        after(g - 1, j - 1)
                run(act, stage, first, last, body)
                prev[0] = (stage, after)

            act.wait_ge(consts_in, 32)
            units = slots_of(S["cq"], 0, 0)
            for i in range(4):
                act.wait_ge(x_gained, i + 1)
                nc.scalar.activation(x_hl[:, 4 * i:4 * i + 4, 0], x_gain[:, 4 * i:4 * i + 4], ACT.Copy)\
                  .then_inc(x_hi, 1)
                unit_to_hi(*units[i])
            for i, (n, slot) in enumerate(slots_of(S["cq"], 1, 1)):
                nc.scalar.activation(x_sq[:, i], x_in[:, 4 * i:4 * i + 4], ACT.Square).then_inc(x_squared, 1)
                unit_to_hi(n, slot)
            root(X_NORM, 4, D)
            low_half(S["cq"], 0, 0)
            prev[0] = (S["cq"], None)
            slots(S["ckv"])
            slots(S["krff"])
            slots(S["fq"], last=1)
            act.wait_ge(scaled, S["krff"].g0)
            nc.scalar.activation(cq_sq[:], cq_z[:], ACT.Square).then_inc(squares_ready, 1)
            nc.scalar.activation(ckv_sq[:], ckv_z[:], ACT.Square).then_inc(squares_ready, 1)
            slots(S["fq"], first=1, last=2)
            root(Q_NORM, 4, Q_LORA)
            root(KV_NORM, 5, KV_LORA)
            slots(S["fq"], first=2, last=3)
            norm_his(Q_NORM, KQ, cq_n, cq_hl, G_Q)
            norm_his(KV_NORM, KKV, ckv_n, ckv_hl, G_KV)
            slots(S["fq"], first=3)
            act.wait_ge(ff_abs, 1)
            nc.scalar.activation(ff_c[FF_A:], ff_b[FF_A:], ACT.Exp, scale=-1.0).then_inc(ff_exp, 1)
            act.wait_ge(ff_exp, 1)
            nc.scalar.activation(ff_b[FF_A:], ff_c[FF_A:], ACT.Ln,
                                 bias=cst[FF_A:, C_ONES:C_ONES + 1]).then_inc(ff_ln, 1)
            slots(S["fk"])
            slots(S["fv"])
            for g in range(8):
                if g == 0:
                    slots(S["gates"], last=1)
                else:
                    slots(S["gates"], first=g, last=g + 1)
                attention_step(g - 1, 0)
            slots(S["gates"], first=8, last=9)
            attention_step(7, 0)

            def two_sigmoids(g, j):
                split_hi(S["gates"], g, j)
                low_half(S["gates"], g - 1, j - 1)
                act.wait_ge(scaled, g + (S["gates"].g0 - 1))
                sigmoids(g - 2)
                sigmoids(g - 9)
            run(act, S["gates"], 9, 16, two_sigmoids)
            slots(S["uq_nope"], last=1)
            act.wait_ge(scaled, S["gates"].g0 + S["gates"].groups - 1)
            sigmoids(S["gates"].groups - 2)
            slots(S["uq_nope"], first=1, last=2)
            act.wait_ge(scaled, S["gates"].g0 + S["gates"].groups)
            sigmoids(S["gates"].groups - 1)
            slots(S["uq_nope"], first=2)
            slots(S["uq_rope"])
            slots(S["ukv_k"])
            slots(S["ukv_v"])
            for g in range(8):
                slots(S["y_fox"], first=g, last=g + 1)
                attention_step(g - 1, 4)
            slots(S["y_mla"], last=1)
            attention_step(7, 4)
            merged = lambda g, j: value_hi(S["y_mla"], g, m_hl)
            slots(S["y_mla"], first=1, after=merged)

            def prepare_hidden(g, j):
                square_resid(S["w_out"], g)
                resid_gain(S["w_out"], g, j, lambda k: hn_hl[:, k, 0], G_MLP, resid_hi)
            slots(S["w_out"], after=prepare_hidden)

            def hidden(stage):
                return lambda g, j: value_hi(stage, g, u_hl)

            def prepare_final(g, j):
                square_resid(down, g)
                resid_gain(down, g, j, lambda k: final_gain[:, k], G_FINAL, gain_done)
            for i in range(MLP_PARTS):
                up, down = S[f"up{i}"], S[f"down{i}"]
                if i == 0:
                    slots(up, last=2)
                    root(MLP_NORM, 4, D)
                    value_hi(up, 0, u_hl)
                    slots(up, first=2, after=hidden(up))
                else:
                    slots(up, after=hidden(up))
                slots(down, after=prepare_final if i == MLP_PARTS - 1 else None)
            low_half(down, down.groups - 1, down.groups - 1)
            prepare_final(down.groups - 1, down.groups - 1)
            root(LAST_NORM, 4, D)

        @block.vector
        def _(dve):
            steps = [0]

            def then_wait(ins):
                steps[0] += 1
                ins.then_inc(vec_step, 1)
                dve.wait_ge(vec_step, steps[0])

            def split_lo(stage, g, j):
                if stage.units == 0.5 and j % 2:
                    return
                for n, slot in slots_of(stage, g, j):
                    unit_to_lo(n, slot)

            def unit_to_lo(n, slot):
                dve.wait_ge(unit_hi, n + 1)
                nc.vector.tensor_tensor(hl[:, slot, :, 1], raw[:, slot], hl[:, slot, :, 0].bitcast(F32),
                                        ALU.subtract).then_inc(unit_split, 1)

            def high_half(stage, g, j):
                b0 = pair_of(stage, j)
                dve.wait_ge(group_low, g + (stage.g0 + 1))
                low, name = part[:, (stage.g0 + j) % 2], stage.name
                two = bass.ds(2 * g, 2)
                dst = {"cq": lambda: cq_z[:, two], "ckv": lambda: ckv_z[:, two],
                       "krff": lambda: kr_z[:], "fq": lambda: fq[:, two], "fk": lambda: fk[:, two],
                       "fv": lambda: v_fox[:, :, bass.ds(COLS * g, COLS)], "gates": lambda: gate[:, two],
                       "uq_nope": lambda: qn[:, two], "uq_rope": lambda: qr_z[:],
                       "ukv_k": lambda: kn[:, two],
                       "ukv_v": lambda: v_mla[:, :, bass.ds(COLS * g, COLS)]}.get(name, lambda: zsum[:])()
                high, total = bank[:, b0:b0 + 2, 0:T], zsum[:]
                if name == "krff":
                    high, low, total = bank[:, b0, 0:T], low[:, 0], zsum[:, 0]
                final_dst = dst
                if name in FROM_X:
                    dst = total
                if name in ("fq", "uq_nope", "uq_rope"):
                    scale = FOX_SCALE if name == "fq" else MLA_SCALE
                    ins = nc.vector.scalar_tensor_tensor(dst, high, scale, low, ALU.mult, ALU.add)
                else:
                    ins = nc.vector.tensor_tensor(dst, high, low, ALU.add)
                ins.then_inc(group_out, 1)
                if name not in FROM_X:
                    return
                summed(stage, g)
                if name == "fv":
                    for tb in range(TB):
                        ins = nc.vector.tensor_scalar(v_fox[:, tb, bass.ds(COLS * g, COLS)], zsum[:, tb],
                                                      rstd_col[:, tb:tb + 1], None, ALU.mult)
                elif name == "krff":
                    ins = nc.vector.tensor_tensor(final_dst, total, rstd[:, X_NORM], ALU.mult)
                else:
                    ins = nc.vector.tensor_tensor(final_dst, total, rstd_both(X_NORM), ALU.mult)
                ins.then_inc(scaled, 1)
                dve.wait_ge(scaled, g + (stage.g0 + 1))

            def rstd_both(norm):
                return rstd[:, norm].unsqueeze(1).broadcast_to([P, 2, T])

            def reciprocal_rms(norm):
                dve.wait_ge(std_done, norm + 1)
                nc.vector.reciprocal(rstd[:, norm], std[:, norm % 2]).then_inc(rstd_ready, 1)
                dve.wait_ge(rstd_ready, norm + 1)

            def summed(stage, g):
                dve.wait_ge(group_out, g + (stage.g0 + 1))

            def norm(norm, kt, src, tmp, dst, gcol):
                reciprocal_rms(norm)
                for j in range(kt // 2):
                    nc.vector.tensor_tensor(tmp[:, 2 * j:2 * j + 2], src[:, 2 * j:2 * j + 2], rstd_both(norm),
                                            ALU.mult).then_inc(normed, 1)
                dve.wait_ge(normed, NORMED0[norm] + kt // 2)
                for k in range(kt):
                    dve.wait_ge(norm_hi, SPLIT0[norm] + k + 1)
                    nc.vector.scalar_tensor_tensor(dst[:, k, 1], tmp[:, k], gain[:, gcol + k:gcol + k + 1],
                                                   dst[:, k, 0].bitcast(F32), ALU.mult,
                                                   ALU.subtract).then_inc(norm_split, 1)

            def sum_resid_squares(stage, g, i):
                n = g + (RESID0[stage.name] - (i * S["down0"].groups) + 1)
                dve.wait_ge(resid_squared, n)
                nc.vector.tensor_tensor(sq_sum[:, i], sq_sum[:, i], sq[:], ALU.add).then_inc(resid_summed, 1)
                dve.wait_ge(resid_summed, n)

            def rotary(z, swap, sin_part, dst, rows, extra):
                for q in range(0, rows, 32):
                    ins = nc.vector.tensor_copy(swap[q:q + 32], z[q ^ 32:(q ^ 32) + 32])
                then_wait(ins)
                shape = [rows, extra, T] if extra else [rows, T]
                table = lambda c: (cst[0:rows, c:c + T].unsqueeze(1).broadcast_to(shape) if extra
                                   else cst[0:rows, c:c + T])
                then_wait(nc.vector.tensor_tensor(sin_part, swap[0:rows], table(C_SIN), ALU.mult))
                then_wait(nc.vector.tensor_tensor(z[0:rows], z[0:rows], table(C_COS), ALU.mult))
                return nc.vector.tensor_tensor(dst, z[0:rows], sin_part, ALU.add)

            def forget_logits():
                f = slice(FF_A, P)
                then_wait(nc.vector.tensor_scalar(ff_a[f], kr_z[f], gain[f, G_FBIAS:G_FBIAS + 1], None, ALU.add))
                then_wait(nc.vector.scalar_tensor_tensor(ff_b[f], ff_a[f], -1.0, ff_a[f], ALU.mult, ALU.max))
                nc.vector.tensor_scalar(ff_a[f], ff_a[f], 0.0, None, ALU.min).then_inc(ff_abs, 1)
                dve.wait_ge(ff_abs, 1)

            def forget_sums():
                f = slice(FF_A, P)
                dve.wait_ge(ff_ln, 1)
                then_wait(nc.vector.tensor_tensor(ff_a[f], ff_a[f], ff_b[f], ALU.subtract))
                then_wait(nc.vector.tensor_tensor_scan(ff_c[f], cst[f, C_ONES:C_ONES + T], ff_a[f], 0.0,
                                                       ALU.mult, ALU.add))
                then_wait(nc.vector.tensor_scalar(left[f], ff_c[f], cst[f, C_LEFT:C_LEFT + 1],
                                                  cst[f, C_LEFT + 1:C_LEFT + 2], ALU.mult, ALU.add))

            def bias_factor(i):
                f = slice(FF_A, P)
                if i:
                    dve.wait_ge(scored, i)
                for hh in range(2):
                    h = 2 * i + hh
                    ins = nc.vector.tensor_scalar(right[f, hh], ff_c[f], cst[f, C_RIGHT_M + h:C_RIGHT_M + h + 1],
                                                  cst[f, C_RIGHT_N + h:C_RIGHT_N + h + 1], ALU.mult, ALU.add)
                ins.then_inc(bias_ready, 1)

            def maxima(i):
                dve.wait_ge(scored, i + 1)
                c = C_MASK_FOX if i < 4 else C_MASK_MLA
                mask = cst[:, c:c + 3 * P].unsqueeze(1).broadcast_to([P, 2, 3 * P])
                then_wait(nc.vector.tensor_tensor(prob[:].rearrange("p h k q -> p h (k q)"), bank[:, 4:6, 0:3 * P],
                                                  mask, ALU.add))
                nc.vector.tensor_reduce(cols[:, 0, 0:2], prob[:, :, 0], AX.X, ALU.max)
                then_wait(nc.vector.tensor_reduce(cols[:, 0, 2:4], prob[:, :, 1:3].rearrange("p h k q -> p h (k q)"),
                                                  AX.X, ALU.max))
                nc.vector.tensor_scalar(cols[:, 1], cols[:, 0], -1.0, None, ALU.mult).then_inc(max_ready, 1)
                if i < 3:
                    bias_factor(i + 1)

            def normalize(i):
                dve.wait_ge(exp_done, 4 * (i + 1))
                then_wait(nc.vector.reciprocal(cols[:, 3], cols[:, 2]))
                for hh in range(2):
                    for q, piece in ((0, slice(0, 1)), (1, slice(1, 3))):
                        c = 2 * q + hh
                        ins = nc.vector.tensor_scalar(prob[:, hh, piece], prob[:, hh, piece],
                                                      cols[:, 3, c:c + 1], None, ALU.mult)
                ins.then_inc(prob_ready, 1)

            def out_lo(i):
                dst = o_fox if i < 4 else o_mla
                dve.wait_ge(o_hi, i + 1)
                h = 2 * (i % 4)
                nc.vector.tensor_tensor(dst[:, h:h + 2, 1], bank[:, 6].rearrange("p (h t) -> p h t", h=2),
                                        dst[:, h:h + 2, 0].bitcast(F32), ALU.subtract).then_inc(o_split, 1)

            def attention_step(step, pair0):
                if step == -1:
                    maxima(pair0)
                    normalize(pair0)
                elif step % 2 == 0:
                    if step < 6:
                        maxima(pair0 + step // 2 + 1)
                        normalize(pair0 + step // 2 + 1)
                else:
                    out_lo(pair0 + step // 2)

            def value_lo(stage, g, dst):
                f = g + FULL0[stage.name]
                dve.wait_ge(full_hi, f + 1)
                nc.vector.tensor_tensor(dst[:, bass.ds(2 * g, 2), 1], full[:],
                                        dst[:, bass.ds(2 * g, 2), 0].bitcast(F32),
                                        ALU.subtract).then_inc(full_split, 1)

            prev = [None]

            def slots(stage, first=0, last=None, after=None):
                last = stage.groups if last is None else last
                if first == 0:
                    split_lo(stage, 0, 0)
                    if prev[0] is not None:
                        p_stage, p_after = prev[0]
                        high_half(p_stage, p_stage.groups - 1, p_stage.groups - 1)
                        if p_after is not None:
                            p_after(p_stage.groups - 1, p_stage.groups - 1)
                    first = 1
                def body(g, j):
                    split_lo(stage, g, j)
                    high_half(stage, g - 1, j - 1)
                    if after is not None:
                        after(g - 1, j - 1)
                run(dve, stage, first, last, body)
                prev[0] = (stage, after)

            units = slots_of(S["cq"], 0, 0)
            for i in range(4):
                q = slice(4 * i, 4 * i + 4)
                dve.wait_ge(x_hi, i + 1)
                nc.vector.tensor_tensor(x_hl[:, q, 1], x_gain[:, q], x_hl[:, q, 0].bitcast(F32),
                                        ALU.subtract).then_inc(x_split, 1)
                unit_to_lo(*units[i])
            units = slots_of(S["cq"], 1, 1)
            unit_to_lo(*units[0])
            dve.wait_ge(x_squared, 2)
            nc.vector.tensor_tensor(x_sq[:, 0], x_sq[:, 0], x_sq[:, 1], ALU.add).then_inc(tree, 1)
            unit_to_lo(*units[1])
            unit_to_lo(*units[2])
            dve.wait_ge(x_squared, 4)
            nc.vector.tensor_tensor(x_sq[:, 2], x_sq[:, 2], x_sq[:, 3], ALU.add).then_inc(tree, 1)
            dve.wait_ge(tree, 2)
            nc.vector.tensor_tensor(x_sq[:, 0], x_sq[:, 0], x_sq[:, 2], ALU.add).then_inc(squares_ready, 1)
            unit_to_lo(*units[3])
            reciprocal_rms(X_NORM)
            high_half(S["cq"], 0, 0)
            prev[0] = (S["cq"], None)
            slots(S["ckv"])
            slots(S["krff"])
            slots(S["fq"], last=1)
            dve.wait_ge(zeroed, 4)
            then_wait(rotary(kr_z, kr_swap, ff_b[0:ROPE], k_rope[0:ROPE, 0], ROPE, 0))
            nc.vector.tensor_copy(k_rope[ROPE:, 1], k_rope[0:ROPE, 0]).then_inc(rope_ready, 1)
            slots(S["fq"], first=1, last=2)
            forget_logits()
            slots(S["fq"], first=2, last=3)
            norm(Q_NORM, KQ, cq_z, cq_n, cq_hl, G_Q)
            norm(KV_NORM, KKV, ckv_z, ckv_n, ckv_hl, G_KV)
            slots(S["fq"], first=3)
            slots(S["fk"])
            dve.wait_ge(rstd_turned, 1)
            then_wait(nc.vector.tensor_copy(rstd_col[:], bank[:, 7, 0:T:P]))
            forget_sums()
            bias_factor(0)
            slots(S["fv"])
            for g in range(8):
                slots(S["gates"], first=g, last=g + 1)
                attention_step(g - 1, 0)
            slots(S["gates"], first=8, last=9)
            attention_step(7, 0)
            slots(S["gates"], first=9)
            slots(S["uq_nope"])

            def turn_queries(g, j):
                summed(S["uq_rope"], g)
                rotary(qr_z, qr_swap, qr_sin[:], qr[:, 2 * g:2 * g + 2], P, 2).then_inc(rope_ready, 1)
                dve.wait_ge(rope_ready, g + 2)
            slots(S["uq_rope"], after=turn_queries)
            slots(S["ukv_k"])
            slots(S["ukv_v"])

            def fox_gated(g, j):
                summed(S["y_fox"], g)
                gs = slice(KT + 2 * g, KT + 2 * g + 2)
                then_wait(nc.vector.tensor_tensor(gate[:, gs], gate[:, gs], zsum[:], ALU.mult))
            dve.wait_ge(gate_done, S["gates"].groups)
            for g in range(8):
                slots(S["y_fox"], first=g, last=g + 1, after=fox_gated)
                attention_step(g - 1, 4)

            def merge(g, j):
                summed(S["y_mla"], g)
                nc.vector.tensor_tensor(zsum[:], zsum[:], gate[:, bass.ds(2 * g, 2)], ALU.mult).then_inc(weighted, 1)
                dve.wait_ge(weighted, g + 1)
                nc.vector.tensor_tensor(full[:], zsum[:], gate[:, bass.ds(2 * g + KT, 2)],
                                        ALU.add).then_inc(full_ready, 1)
                dve.wait_ge(full_ready, g + 1)
                value_lo(S["y_mla"], g, m_hl)
            slots(S["y_mla"], last=1)
            attention_step(7, 4)
            slots(S["y_mla"], first=1, after=merge)

            def add_resid(stage):
                def after(g, j):
                    summed(stage, g)
                    two = bass.ds(2 * g, 2)
                    nc.vector.tensor_tensor(resid[:, two], resid[:, two], zsum[:], ALU.add).then_inc(resid_done, 1)
                    dve.wait_ge(resid_done, g + (RESID0[stage.name] + 1))
                    if stage.name == "w_out":
                        for b in range(2):
                            one = bass.ds(2 * g + b, 1)
                            dve.wait_ge(resid_hi, g * 2 + (b + 1))
                            ins = nc.vector.scalar_tensor_tensor(
                                hn_hl[:, one, 1], resid[:, one], gain[:, bass.ds(2 * g + (G_MLP + b), 1)],
                                hn_hl[:, one, 0].bitcast(F32), ALU.mult, ALU.subtract)
                        ins.then_inc(resid_split, 1)
                        sum_resid_squares(stage, g, 0)
                    elif stage.name == "down1":
                        sum_resid_squares(stage, g, 1)
                return after
            dve.wait_ge(resid_in, 16)
            slots(S["w_out"], after=add_resid(S["w_out"]))

            def hidden(stage):
                def after(g, j):
                    summed(stage, g)
                    f = g + FULL0[stage.name]
                    nc.vector.scalar_tensor_tensor(relu[:], zsum[:], 0.0, rstd_both(MLP_NORM), ALU.max,
                                                   ALU.mult).then_inc(relu_ready, 1)
                    dve.wait_ge(relu_ready, f + (1 - FULL0["up0"]))
                    value_lo(stage, g, u_hl)
                return after
            for i in range(MLP_PARTS):
                up, down = S[f"up{i}"], S[f"down{i}"]
                if i == 0:
                    slots(up, last=1)
                    slots(up, first=1, last=2)
                    reciprocal_rms(MLP_NORM)
                    hidden(up)(0, 0)
                    slots(up, first=2, after=hidden(up))
                else:
                    slots(up, after=hidden(up))
                slots(down, after=add_resid(down))
            high_half(down, down.groups - 1, down.groups - 1)
            add_resid(down)(down.groups - 1, down.groups - 1)
            reciprocal_rms(LAST_NORM)
            for k in range(0, KT, 2):
                dve.wait_ge(gain_done, k + 2)
                nc.vector.tensor_tensor(final[:, k:k + 2], final_gain[:, k:k + 2], rstd_both(LAST_NORM),
                                        ALU.mult).then_inc(final_done, 1)


def pack_stream(w_in, w_uq, w_ukv, w_mla_branch, w_fox_branch, w_out, w_up, w_down):
    stream = np.empty((N_UNITS, P, SLABS, COLS), w_in.dtype)
    at = [0]

    def columns(w, k_first=0, k_count=None):
        k_count = w.shape[0] // P if k_count is None else k_count
        w = w[k_first * P:(k_first + k_count) * P]
        groups = w.shape[1] // COLS
        units = (k_count // SLABS) * groups
        v = w.reshape(k_count // SLABS, SLABS, P, groups, COLS)
        stream[at[0]:at[0] + units] = v.transpose(3, 0, 2, 1, 4).reshape(units, P, SLABS, COLS)
        at[0] += units

    def half_units(w):
        v = w.reshape(2, P, w.shape[1] // COLS // 2, 2, COLS)
        units = w.shape[1] // COLS // 2
        stream[at[0]:at[0] + units] = v.transpose(2, 1, 3, 0, 4).reshape(units, P, SLABS, COLS)
        at[0] += units

    columns(w_in[:, 0:OFF_CKV])
    columns(w_in[:, OFF_CKV:OFF_KR])
    forget = w_in[:, OFF_FF:OFF_FF + 32]
    narrow = np.concatenate([w_in[:, OFF_KR:OFF_FQ], forget, forget], axis=1)
    v = narrow.reshape(KT // SLABS // 2, SLABS, 2, P, P)
    stream[at[0]:at[0] + 2] = v.transpose(0, 3, 1, 2, 4).reshape(2, P, SLABS, COLS)
    at[0] += 2
    for first in (OFF_FQ, OFF_FK, OFF_FV):
        columns(w_in[:, first:first + HEADS * DH])
    columns(w_in[:, OFF_G:])
    uq = w_uq.reshape(Q_LORA, HEADS, DH + ROPE)
    columns(uq[:, :, :DH].reshape(Q_LORA, HEADS * DH))
    columns(uq[:, :, DH:].reshape(Q_LORA, HEADS * ROPE))
    ukv = w_ukv.reshape(KV_LORA, HEADS, 2, DH)
    half_units(ukv[:, :, 0].reshape(KV_LORA, HEADS * DH))
    half_units(ukv[:, :, 1].reshape(KV_LORA, HEADS * DH))
    columns(w_fox_branch)
    columns(w_mla_branch)
    columns(w_out)
    per = D_FF // MLP_PARTS
    for i in range(MLP_PARTS):
        columns(w_up[:, i * per:(i + 1) * per])
        columns(w_down, i * per // P, per // P)
    assert at[0] == N_UNITS
    return stream


def kernel(x, attn_norm, w_in, fox_f_bias, q_norm, w_uq, kv_norm, w_ukv,
           w_mla_branch, w_fox_branch, w_out, mlp_norm, w_up, w_down, final_norm):
    import concourse.bacc as bacc
    from concourse.bass_utils import run_bass_kernel_spmd

    a = np.asarray
    stream = pack_stream(a(w_in)[0], a(w_uq)[0], a(w_ukv)[0], a(w_mla_branch)[0], a(w_fox_branch)[0],
                         a(w_out)[0], a(w_up)[0], a(w_down)[0])
    x_t = np.ascontiguousarray(a(x)[0].T.reshape(KT, P, T).transpose(1, 0, 2))
    gains = np.zeros((P, G_COUNT), np.float32)
    for col, g in ((G_ATTN, a(attn_norm)[0]), (G_Q, a(q_norm)[0]), (G_KV, a(kv_norm)[0]),
                   (G_MLP, a(mlp_norm)[0]), (G_FINAL, a(final_norm))):
        gains[:, col:col + g.size // P] = g.reshape(-1, P).T
    for row in (FF_A, FF_B):
        gains[row:row + HEADS, G_FBIAS] = a(fox_f_bias)[0]

    nc = bacc.Bacc("TRN2", target_bir_lowering=False, num_devices=1)
    arrays = {"weights": stream, "x_t": x_t, "consts": constants(), "gains": gains}
    aps = [nc.dram_tensor(k, v.shape, F32, kind="ExternalInput").ap() for k, v in arrays.items()]
    out_t = nc.dram_tensor("out_t", (P, KT, T), F32, kind="ExternalOutput").ap()
    program(nc, *aps, out_t)
    r = run_bass_kernel_spmd(nc, [arrays], core_ids=[0])
    y = r.results[0]["out_t"]
    return np.ascontiguousarray(y.transpose(1, 0, 2).reshape(D, T).T)[None]
```

```python
import math
from contextlib import ExitStack

import numpy as np
import concourse.bass as bass
from concourse import mybir

F32 = mybir.dt.float32
F32R = mybir.dt.float32r
ALU = mybir.AluOpType
ACT = mybir.ActivationFunctionType
AX = mybir.AxisListType

P = 128
D = 2048
T = 256
TB = T // P
CHUNK = 64
HEADS = 8
DH = 128
ROPE = 64
Q_LORA, KV_LORA = 512, 256
D_FF = 4 * D
ROPE_THETA = 10000.0
EPS = 1e-6
KT = D // P
KQ, KKV = Q_LORA // P, KV_LORA // P

OFF_CKV = Q_LORA
OFF_KR = OFF_CKV + KV_LORA
OFF_FQ = OFF_KR + ROPE
OFF_FK = OFF_FQ + HEADS * DH
OFF_FV = OFF_FK + HEADS * DH
OFF_FF = OFF_FV + HEADS * DH
OFF_G = OFF_FF + HEADS

SLABS, COLS = 4, 256
RING = 4
WARM_UPS = 6
MLP_PARTS = 2
FF_GROUPS = D_FF // COLS // MLP_PARTS

FOX_SCALE = 1.0 / math.sqrt(DH)
MLA_SCALE = 1.0 / math.sqrt(DH + ROPE)
MASKED = -3.0e38

FF = ROPE


class Stage:
    def __init__(self, name, groups, units):
        self.name, self.groups, self.units = name, groups, units
        self.g0 = self.u0 = 0


def make_stages():
    stages = [
        Stage("cq", Q_LORA // COLS, KT // SLABS),
        Stage("ckv", KV_LORA // COLS, KT // SLABS),
        Stage("krff", 1, KT // SLABS // 2),
        Stage("fq", HEADS * DH // COLS, KT // SLABS),
        Stage("fk", HEADS * DH // COLS, KT // SLABS),
        Stage("fv", HEADS * DH // COLS, KT // SLABS),
        Stage("gates", 2 * D // COLS, KT // SLABS),
        Stage("uq_nope", HEADS * DH // COLS, KQ // SLABS),
        Stage("uq_rope", HEADS * ROPE // COLS, KQ // SLABS),
        Stage("ukv_k", HEADS * DH // COLS, 0.5),
        Stage("ukv_v", HEADS * DH // COLS, 0.5),
        Stage("y_fox", D // COLS, HEADS // SLABS),
        Stage("y_mla", D // COLS, HEADS // SLABS),
        Stage("w_out", D // COLS, KT // SLABS),
    ]
    for part in range(MLP_PARTS):
        stages.append(Stage(f"up{part}", FF_GROUPS, KT // SLABS))
        stages.append(Stage(f"down{part}", D // COLS, D_FF // P // MLP_PARTS // SLABS))
    g = u = 0
    for s in stages:
        s.g0, s.u0 = g, u
        g += s.groups
        u += int(s.groups * s.units)
    return stages, g, u


STAGES, N_GROUPS, N_UNITS = make_stages()
S = {s.name: s for s in STAGES}
assert N_UNITS % RING == 0


def make_due():
    due = [[] for _ in range(N_UNITS)]
    for s in STAGES:
        lead = RING if s.units > 1 else RING - 1
        for g in range(s.groups):
            last = s.u0 + (g // 2 if s.units == 0.5 else (g + 1) * s.units - 1)
            due[min(last + lead, N_UNITS - 1)].append((s, g))
    return due


DUE = make_due()

C_IDENT = 0
C_MASK_FOX = C_IDENT + P
C_MASK_MLA = C_MASK_FOX + 3 * P
C_COS = C_MASK_MLA + 3 * P
C_SIN = C_COS + T
C_ONE = C_SIN + T
C_PART = C_ONE + 1
C_LEFT = C_PART + 2
C_RIGHT_M = C_LEFT + 2
C_RIGHT_N = C_RIGHT_M + HEADS
C_EPS = C_RIGHT_N + HEADS
C_COUNT = C_EPS + 1

G_ATTN = 0
G_Q = G_ATTN + KT
G_KV = G_Q + KQ
G_MLP = G_KV + KKV
G_FINAL = G_MLP + KT
G_FBIAS = G_FINAL + KT
G_COUNT = G_FBIAS + 1


def constants():
    c = np.zeros((P, C_COUNT), np.float32)
    p = np.arange(P)
    c[:, C_IDENT:C_IDENT + P] = np.eye(P)
    for col, keep in ((C_MASK_FOX, p[None, :] <= p[:, None]),
                      (C_MASK_MLA, p[None, :] // CHUNK <= p[:, None] // CHUNK)):
        diagonal = np.where(keep, 0.0, MASKED)
        c[:, col:col + P] = diagonal
        c[:, col + 2 * P:col + 3 * P] = diagonal
    half = ROPE // 2
    inv = np.float32(1.0) / np.power(np.float32(ROPE_THETA),
                                     np.arange(0, ROPE, 2, dtype=np.float32) / np.float32(ROPE))
    angle = (inv[p % half][:, None] * np.arange(T, dtype=np.float32)[None, :]).astype(np.float32)
    c[:, C_COS:C_COS + T] = np.cos(angle)
    c[:, C_SIN:C_SIN + T] = np.where(p % ROPE < half, -1.0, 1.0)[:, None] * np.sin(angle)
    c[:, C_ONE] = 1.0
    copy = lambda n: slice(FF + n * HEADS, FF + (n + 1) * HEADS)
    for n in range(4):
        c[copy(n), C_PART + n % 2] = 1.0
        c[copy(n), C_LEFT + (0 if n >= 2 else 1)] = 1.0
        if n < 2:
            c[copy(n), C_RIGHT_M:C_RIGHT_M + HEADS] = -np.eye(HEADS)
        else:
            c[copy(n), C_RIGHT_N:C_RIGHT_N + HEADS] = np.eye(HEADS)
    c[:, C_EPS] = EPS
    return c


def program(nc, stream, x_t, consts, gains, out_t):
    sbuf0 = (nc.sbuf_base + 511) // 512 * 512
    kib = 1024

    def at(name, offset, *shape, dt=F32):
        return nc.alloc_sbuf_tensor_at(name, [P, *shape], dt, offset=sbuf0 + offset)

    raw = at("raw", 0, RING, SLABS, COLS)
    hl = at("hl", 16 * kib, RING, SLABS, 2, COLS, dt=F32R)
    H = 48 * kib
    o_fox = at("o_fox", H, HEADS, 2, T, dt=F32R)
    resid = at("resid", H, KT, T)
    o = H + 16 * kib
    cst = at("cst", o, C_COUNT)
    gain = at("gain", o + 8 * kib, G_COUNT)
    cols = at("cols", o + 8 * kib + 512, 4, 4)
    part = at("part", o + 9 * kib, 2, 2, T)
    zsum = at("zsum", o + 13 * kib, 2, T)
    pair_sum = at("pair_sum", o + 13 * kib, 2, 2, T)
    prob = at("prob", o + 19 * kib, 2, 3, P)
    prob_t = at("prob_t", o + 22 * kib, 2, 3, P)
    full = at("full", o + 19 * kib, 2, 2, T)
    relu = at("relu", o + 17 * kib, 2, T)
    assert C_COUNT * 4 <= 8 * kib and G_COUNT * 4 <= 512
    A = o + 25 * kib
    x_hl = at("x_hl", A, KT, 2, T, dt=F32R)
    qn = at("qn", A, HEADS, T)
    kn = at("kn", A + 8 * kib, HEADS, T)
    v_mla = at("v_mla", A + 16 * kib, TB, HEADS * DH)
    qr = at("qr", A + 24 * kib, HEADS // 2, T)
    m_hl = at("m_hl", A, KT, 2, T, dt=F32R)
    B = A + 32 * kib
    fq = at("fq", B, HEADS, T)
    fk = at("fk", B + 8 * kib, HEADS, T)
    v_fox = at("v_fox", B + 16 * kib, TB, HEADS * DH)
    cq_hl = at("cq_hl", B + 24 * kib, KQ, 2, T, dt=F32R)
    o_mla = at("o_mla", B, HEADS, 2, T, dt=F32R)
    qr_z = at("qr_z", B + 16 * kib, 2, 2, T)
    qr_swap = at("qr_swap", B + 20 * kib, 2, 2, T)
    x_sq = at("x_sq", B, 4, 4, T)
    u_hl = at("u_hl", A, D_FF // P // MLP_PARTS, 2, T, dt=F32R)
    C = B + 32 * kib
    x_in = at("x_in", C, KT, T)
    gate = at("gate", C, 2 * KT, T)
    cq_z = at("cq_z", C, KQ, T)
    ckv_z = at("ckv_z", C + 4 * kib, KKV, T)
    cq_sq = at("cq_sq", C + 6 * kib, KQ, T)
    ckv_sq = at("ckv_sq", C + 10 * kib, KKV, T)
    cq_n = at("cq_n", C + 12 * kib, KQ, T)
    ckv_n = at("ckv_n", C + 16 * kib, KKV, T)
    kr_z = at("kr_z", C + 18 * kib, T)
    kr_swap = at("kr_swap", C + 19 * kib, T)
    ff_a = at("ff_a", C + 20 * kib, T)
    ff_b = at("ff_b", C + 21 * kib, T)
    ff_c = at("ff_c", C + 22 * kib, T)
    ff_hi = at("ff_hi", C + 23 * kib, T, dt=F32R)
    final_gain = at("final_gain", C, KT, T)
    final = at("final", C + 16 * kib, KT, T)
    hn_hl = at("hn_hl", C, KT, 2, T, dt=F32R)
    E = C + 32 * kib
    ckv_hl = at("ckv_hl", E, KKV, 2, T, dt=F32R)
    k_rope = at("k_rope", E + 4 * kib, 2, T)
    left = at("left", E + 6 * kib, T, dt=F32R)
    right = at("right", E + 7 * kib, 2, T, dt=F32R)
    rstd = at("rstd", E + 9 * kib, 5, T)
    std_col = at("std_col", E + 14 * kib, 5, TB)
    rstd_col = at("rstd_col", E + 14 * kib + 64, 5, TB)
    sq = at("sq", E + 15 * kib, 2, T)
    sq_sum = at("sq_sum", E + 17 * kib, 2, 2, T)
    assert sbuf0 + E + 21 * kib <= nc.sbuf_usable_end, (sbuf0 + E + 21 * kib, nc.sbuf_usable_end)

    ctx = ExitStack()
    with ctx:
        sem = lambda name: ctx.enter_context(nc.semaphore(name))
        bank = ctx.enter_context(nc.psum_tensor("bank", [P, 8, 512], F32))

        unit_loaded = [sem(f"unit_loaded{i}") for i in range(RING)]
        unit_hi = sem("unit_hi")
        unit_split = sem("unit_split")
        halves_used = sem("halves_used")
        group_low = sem("group_low")
        group_out = sem("group_out")
        consts_in = sem("consts_in")
        x_loaded = [sem(f"x_loaded{i}") for i in range(4)]
        X_LOADED = (32, 16, 16, 16)
        resid_in = sem("resid_in")
        zeroed = sem("zeroed")
        x_hi = sem("x_hi")
        x_split = sem("x_split")
        x_squared = sem("x_squared")
        qkv_squared = sem("qkv_squared")
        squares_ready = sem("squares_ready")
        squares_summed = sem("squares_summed")
        std_done = sem("std_done")
        rstd_col_done = sem("rstd_col_done")
        rstd_spread = sem("rstd_spread")
        rstd_ready = sem("rstd_ready")
        scaled = sem("scaled")
        normed = sem("normed")
        norm_hi = sem("norm_hi")
        norm_split = sem("norm_split")
        rope_ready = sem("rope_ready")
        pair_used = sem("pair_used")
        ff_exp = sem("ff_exp")
        ff_ln = sem("ff_ln")
        ff_abs = sem("ff_abs")
        bias_ready = sem("bias_ready")
        scored = sem("scored")
        max_ready = sem("max_ready")
        exp_done = sem("exp_done")
        prob_ready = sem("prob_ready")
        transposed = sem("transposed")
        prob_t_ready = sem("prob_t_ready")
        mixed = sem("mixed")
        o_hi = sem("o_hi")
        o_split = sem("o_split")
        gate_done = sem("gate_done")
        full_ready = sem("full_ready")
        full_hi = sem("full_hi")
        full_split = sem("full_split")
        relu_ready = sem("relu_ready")
        resid_done = sem("resid_done")
        last_done = sem("last_done")
        resid_squared = sem("resid_squared")
        resid_summed = sem("resid_summed")
        resid_hi = sem("resid_hi")
        resid_split = sem("resid_split")
        gain_done = sem("gain_done")
        final_done = sem("final_done")
        stored = sem("stored")
        vec_step = sem("vec_step")
        pool_step = sem("pool_step")
        qr_swapped = sem("qr_swapped")

        block = ctx.enter_context(nc.Block())

        FULL0 = {"y_mla": 0}
        for i in range(MLP_PARTS):
            FULL0[f"up{i}"] = S["y_mla"].groups + i * FF_GROUPS
        X_NORM, Q_NORM, KV_NORM, MLP_NORM, LAST_NORM = range(5)
        NORMED0 = {Q_NORM: 0, KV_NORM: KQ // 2}
        SPLIT0 = {Q_NORM: 0, KV_NORM: KQ}
        RESID0 = {"w_out": 0, "down0": S["w_out"].groups, "down1": 2 * S["w_out"].groups}
        OUT_PIECES = [slice(0, 1), *(slice(k, k + 2) for k in range(1, KT - 1, 2)), slice(KT - 1, KT)]
        FROM_X = ("cq", "ckv", "krff", "fq", "fk", "fv", "gates")

        SHORT0, SHORT_GROUPS = S["uq_nope"].g0, S["y_fox"].g0 - S["uq_nope"].g0

        def run(eng, stage, first, last, body):
            if 2 * stage.units % RING:
                for g in range(first, last):
                    body(g, g)
                return
            if (last - first) % 2:
                body(first, first)
                first += 1
            if last - first == 2:
                body(first, first)
                body(first + 1, first + 1)
            elif last > first:
                with eng.Fori(0, (last - first) // 2) as i:
                    body(i * 2 + first, first)
                    body(i * 2 + (first + 1), first + 1)

        def slots_of(stage, g, j):
            if stage.units == 0.5:
                return [(stage.u0 + g // 2, (stage.u0 + j // 2) % RING)]
            n = stage.units
            return [(g * n + (stage.u0 + k), (stage.u0 + j * n + k) % RING) for k in range(n)]

        def unit_index(stage, g, k):
            return stage.u0 + g // 2 if stage.units == 0.5 else stage.u0 + g * stage.units + k

        LOOP_FROM = {"fk": 2, "gates": 10, "y_mla": 3, "up0": 2}

        def walk(eng, split, take):
            for stage in STAGES:
                def turn(g, j, stage=stage):
                    if stage.units == 0.5 and j % 2:
                        return
                    for k in range(max(1, int(stage.units))):
                        split(stage, g, j, k)
                        for s, gone in DUE[unit_index(stage, j, k)]:
                            take(s, gone if isinstance(g, int) else g - (j - gone), gone)

                first = LOOP_FROM.get(stage.name, 0)
                while first < stage.groups and any(
                        s is not stage for k in range(max(1, int(stage.units)))
                        for s, _ in DUE[unit_index(stage, first, k)]):
                    first += 1
                if stage.name in ("cq", "fq", "y_fox"):
                    first = stage.groups
                last = stage.groups - (2 if stage is STAGES[-1] else 0)
                for g in range(min(first, stage.groups)):
                    turn(g, g)
                if first < last:
                    run(eng, stage, first, last, turn)
                    first = last
                for g in range(first, stage.groups):
                    turn(g, g)

        def pair_of(stage, j):
            n = stage.g0 + j - SHORT0
            if 0 <= n < 4:
                return (4, 6, 0, 2)[n]
            if 4 <= n < SHORT_GROUPS:
                return 2 * (n % 4)
            return 2 * ((stage.g0 + j) % 2)

        def wait_for_banks(pe, stage, g, j):
            n = stage.g0 + j - SHORT0
            if 0 <= n < 2:
                pe.wait_ge(o_split, HEADS // 2)
            elif n in (2, 3) or 6 <= n < SHORT_GROUPS:
                pe.wait_ge(group_out, g + (stage.g0 - 3))
            elif stage.g0 + j >= 2:
                pe.wait_ge(group_out, g + (stage.g0 - 1))

        assert pair_of(S['ukv_v'], 0) == 4

        def halves_until(stage, g):
            halves = int(2 * stage.units)
            return g * halves + (int(2 * stage.u0) + halves)

        @block.sync
        def _(sp):
            for n in range(RING):
                sp.dma_start(raw[:, n], stream[n]).then_inc(unit_loaded[n], 16)
                sp.dma_start(x_in[:, 4 * n:4 * n + 4], x_t[:, 4 * n:4 * n + 4]).then_inc(x_loaded[n], 16)
            with sp.Fori(1, N_UNITS // RING) as turn:
                for k in range(RING):
                    sp.wait_ge(unit_split, turn * RING + (k + 1 - RING))
                    sp.dma_start(raw[:, k], stream[bass.ds(turn * RING + k, 1)].rearrange("a p s c -> p (a s) c"))\
                      .then_inc(unit_loaded[k], 16)
            for i, tiles in enumerate(OUT_PIECES):
                sp.wait_ge(final_done, i + 1)
                sp.dma_start(out_t[:, tiles], final[:, tiles]).then_inc(stored, 16)
            sp.wait_ge(stored, 16 * len(OUT_PIECES))

        @block.gpsimd
        def _(pool):
            nc.gpsimd.memset(k_rope[:], 0.0).then_inc(zeroed, 1)
            for i in range(4):
                x4 = x_in[:, 4 * i:4 * i + 4]
                pool.wait_ge(x_loaded[i], X_LOADED[i])
                nc.gpsimd.tensor_tensor(x_sq[:, i], x4, x4, ALU.mult).then_inc(x_squared, 1)
            pool.wait_ge(x_squared, 4)
            nc.gpsimd.tensor_tensor(x_sq[:, 0], x_sq[:, 0], x_sq[:, 1], ALU.add).then_inc(x_squared, 1)
            nc.gpsimd.memset(sq_sum[:], 0.0).then_inc(zeroed, 1)
            nc.gpsimd.memset(left[:].bitcast(F32), 0.0).then_inc(zeroed, 1)
            nc.gpsimd.memset(right[:].bitcast(F32), 0.0).then_inc(zeroed, 1)
            pool.wait_ge(qkv_squared, 1)
            nc.gpsimd.tensor_tensor(cq_sq[:, 0:2], cq_sq[:, 0:2], cq_sq[:, 2:4], ALU.add).then_inc(pool_step, 1)
            pool.wait_ge(pool_step, 1)
            nc.gpsimd.tensor_tensor(cq_sq[:, 0], cq_sq[:, 0], cq_sq[:, 1], ALU.add).then_inc(squares_ready, 1)
            pool.wait_ge(qkv_squared, 2)
            nc.gpsimd.tensor_tensor(ckv_sq[:, 0], ckv_sq[:, 0], ckv_sq[:, 1], ALU.add).then_inc(squares_ready, 1)
            for g in range(2):
                pool.wait_ge(qr_swapped, g + 1)
                table = lambda c: cst[:, c:c + T].unsqueeze(1).broadcast_to([P, 2, T])
                nc.gpsimd.tensor_tensor(qr_swap[:, g], qr_swap[:, g], table(C_SIN), ALU.mult).then_inc(pool_step, 1)
                nc.gpsimd.tensor_tensor(qr_z[:, g], qr_z[:, g], table(C_COS), ALU.mult).then_inc(pool_step, 1)
                pool.wait_ge(pool_step, 2 * (g + 1) + 1)
                nc.gpsimd.tensor_tensor(qr[:, 2 * g:2 * g + 2], qr_z[:, g], qr_swap[:, g],
                                        ALU.add).then_inc(rope_ready, 1)
            pool.wait_ge(gate_done, S["gates"].groups)
            for g in range(S["y_fox"].groups):
                gs = slice(KT + 2 * g, KT + 2 * g + 2)
                pool.wait_ge(group_out, S["y_fox"].g0 + g + 1)
                nc.gpsimd.tensor_tensor(gate[:, gs], gate[:, gs], pair_sum[:, g % 2], ALU.mult).then_inc(pair_used, 1)
            pool.wait_ge(halves_used, halves_until(S["y_fox"], S["y_fox"].groups - 1))
            pool.dma_start(resid[:], x_t).then_inc(resid_in, 16)
            done = S["y_fox"].groups
            pool.wait_ge(pair_used, done)
            for g in range(S["y_mla"].groups):
                pool.wait_ge(group_out, S["y_mla"].g0 + g + 1)
                gs = slice(2 * g, 2 * g + 2)
                nc.gpsimd.tensor_tensor(gate[:, gs], gate[:, gs], pair_sum[:, g % 2], ALU.mult).then_inc(pair_used, 1)
                pool.wait_ge(pair_used, done + g + 1)
                if g >= 2:
                    pool.wait_ge(full_split, g - 1)
                nc.gpsimd.tensor_tensor(full[:, g % 2], gate[:, gs], gate[:, KT + 2 * g:KT + 2 * g + 2],
                                        ALU.add).then_inc(full_ready, 1)

        @block.tensor
        def _(pe):
            def norm_sum(norm, b, tiles):
                if norm == MLP_NORM:
                    pe.wait_ge(resid_summed, S["w_out"].groups)
                else:
                    pe.wait_ge(squares_ready, norm + 1)
                for tb in range(TB):
                    for i, tile in enumerate(tiles):
                        last = nc.tensor.matmul(bank[:, b, T + tb:T + tb + 1], tile[:, tb * P:tb * P + P],
                                                cst[:, C_ONE:C_ONE + 1], start=i == 0, stop=i == len(tiles) - 1)
                last.then_inc(squares_summed, 1)

            def last_norm_sum():
                tiles = [sq_sum[:, 1, 0], sq_sum[:, 1, 1], sq[:, 0], sq[:, 1]]
                for i, tile in enumerate(tiles):
                    pe.wait_ge(resid_summed, 2 * S["w_out"].groups - 1 + max(0, i - 1))
                    for tb in range(TB):
                        last = nc.tensor.matmul(bank[:, 6 + tb, 0:1], tile[:, tb * P:tb * P + P],
                                                cst[:, C_ONE:C_ONE + 1], start=i == 0, stop=i == len(tiles) - 1)
                last.then_inc(squares_summed, 1)

            def spread(norm, b):
                pe.wait_ge(rstd_col_done, norm + 1)
                for tb in range(TB):
                    last = nc.tensor.transpose(bank[:, b, tb * P:tb * P + P],
                                               rstd_col[:, norm, tb:tb + 1].broadcast_to([P, P]),
                                               cst[:, C_IDENT:C_IDENT + P])
                last.then_inc(rstd_spread, 1)

            def product(ps, slot, s, col, x, first, end):
                nc.tensor.matmul(ps, hl[:, slot, s, 0, col:col + P], x.rearrange("p h t -> p (h t)"),
                                 start=first, stop=False)
                return nc.tensor.matmul(ps[:, T:], hl[:, slot, s, 1, col:col + P], x[:, 0], start=False, stop=end)

            def group(stage, g, j, moving, k_tiles, values=False, narrow=False, ready=None, at_tile=None):
                b0 = pair_of(stage, j)
                wait_for_banks(pe, stage, g, j)
                k = 0
                units = slots_of(stage, g, j)
                for ui, (n, slot) in enumerate(units):
                    pe.wait_ge(unit_split, n + 1)
                    slabs = range(SLABS)
                    if stage.units == 0.5:
                        slabs = range(2 * (j % 2), 2 * (j % 2) + 2)
                    if ready is not None:
                        ready(ui)
                    if stage is STAGES[-1] and j == stage.groups - 1 and ui == len(units) - 1:
                        for b in range(2):
                            for s in slabs:
                                last = product(bank[:, b0 + b], slot, s, P * b, moving(k + s), False, s == SLABS - 1)
                            last.then_inc(halves_used, 1)
                        k += SLABS
                        continue
                    for s in slabs:
                        for sub in range(2 if narrow else 1):
                            if at_tile is not None:
                                at_tile(k)
                            x = moving(k)
                            first, end = k == 0, k == k_tiles - 1
                            for b in range(1 if narrow else 2):
                                ps = bank[:, b0 + b]
                                if values:
                                    tok = slice(b * P, b * P + P)
                                    nc.tensor.matmul(ps, x[:, 0, tok], hl[:, slot, s].rearrange("p h c -> p (h c)"),
                                                     start=first, stop=False)
                                    last = nc.tensor.matmul(ps[:, T:], x[:, 1, tok], hl[:, slot, s, 0],
                                                            start=False, stop=end)
                                else:
                                    last = product(ps, slot, s, P * (sub if narrow else b), x, first, end)
                            k += 1
                        if s % 2:
                            last.then_inc(halves_used, 1)
                assert k == k_tiles

            def x_ready(k):
                pe.wait_ge(x_split, k + 1)

            def x_norm(k):
                if k == 6:
                    pe.wait_ge(consts_in, 16)
                    norm_sum(X_NORM, 4, [x_sq[:, 0, i] for i in range(2)])
                elif k == 11:
                    spread(X_NORM, 4)

            def spread_q_kv(ui):
                if ui == 3:
                    spread(Q_NORM, 4)
                    spread(KV_NORM, 5)

            def resid_ready(ui):
                pe.wait_ge(resid_split, 2 * (ui + 1))
                if ui == 3:
                    norm_sum(MLP_NORM, 4, [sq_sum[:, 0, k] for k in range(2)])

            def spread_mlp(ui):
                if ui == 0:
                    spread(MLP_NORM, 4)

            def plain(stage, tile, k_tiles, first=0, last=None, **kw):
                last = stage.groups if last is None else last
                def body(g, j):
                    group(stage, g, j, lambda k: tile[:, k], k_tiles, **kw)
                run(pe, stage, first, last, body)

            def scores(i, branch):
                done = i + 4 * (branch == "mla")
                if done:
                    pe.wait_ge(max_ready, done)
                if branch == "fox":
                    pe.wait_ge(bias_ready, i + 1)
                else:
                    pe.wait_ge(rope_ready, 2 + i // 2)
                for hh in range(2):
                    h = 2 * i + hh
                    for qs, ks, c0 in ((slice(0, P), slice(0, P), 0), (slice(P, T), slice(0, T), P)):
                        dst = bank[:, 4 + hh, c0:c0 + ks.stop]
                        if branch == "fox":
                            nc.tensor.matmul(dst, fq[:, h, qs], fk[:, h, ks], start=True, stop=False)
                            last = nc.tensor.matmul(dst, left[:, qs], right[:, hh, ks], start=False, stop=True)
                        else:
                            nc.tensor.matmul(dst, qn[:, h, qs], kn[:, h, ks], start=True, stop=False)
                            last = nc.tensor.matmul(dst, qr[:, i, qs], k_rope[:, hh, ks], start=False, stop=True)
                last.then_inc(scored, 1)

            def transposes(i, branch):
                done = i + 4 * (branch == "mla")
                pe.wait_ge(prob_ready, done + 1)
                if done:
                    pe.wait_ge(o_split, done)
                for hh in range(2):
                    for piece in range(3):
                        last = nc.tensor.transpose(bank[:, 6 + hh, piece * P:piece * P + P],
                                                   prob[:, hh, piece], cst[:, C_IDENT:C_IDENT + P])
                last.then_inc(transposed, 1)

            def mix(i, branch):
                v = v_fox if branch == "fox" else v_mla
                if i == 0 and branch == "fox":
                    pe.wait_ge(scaled, S["fv"].g0 + S["fv"].groups)
                elif i == 0:
                    pe.wait_ge(group_out, S["ukv_v"].g0 + S["ukv_v"].groups)
                pe.wait_ge(prob_t_ready, i + 4 * (branch == "mla") + 1)
                for hh in range(2):
                    cs = slice((2 * i + hh) * DH, (2 * i + hh + 1) * DH)
                    nc.tensor.matmul(bank[:, 6, hh * T:hh * T + T], v[:, 0, cs],
                                     prob_t[:, hh, 0:2].rearrange("p b q -> p (b q)"), start=True, stop=False)
                    last = nc.tensor.matmul(bank[:, 6, hh * T + P:hh * T + T], v[:, 1, cs],
                                            prob_t[:, hh, 2], start=False, stop=True)
                last.then_inc(mixed, 1)

            def attend(stage, tile, k_tiles, branch, **kw):
                scores(0, branch)
                for g in range(8):
                    group(stage, g, g, lambda k: tile[:, k], k_tiles, **kw)
                    if g % 2 == 0:
                        transposes(g // 2, branch)
                        if g < 6:
                            scores(g // 2 + 1, branch)
                    else:
                        mix(g // 2, branch)

            pe.wait_ge(zeroed, 1)
            for _ in range(WARM_UPS):
                nc.tensor.matmul(bank[:, 7, 0:T], k_rope[:, 0, 0:P], k_rope[:, 1], start=True, stop=True)
            plain(S["cq"], x_hl, KT, last=1, at_tile=x_ready)
            plain(S["cq"], x_hl, KT, first=1, at_tile=x_norm)
            plain(S["ckv"], x_hl, KT)
            plain(S["krff"], x_hl, KT, narrow=True)
            plain(S["fq"], x_hl, KT, last=1)
            pe.wait_ge(rstd_ready, X_NORM + 1)
            norm_sum(Q_NORM, 4, [cq_sq[:, 0]])
            norm_sum(KV_NORM, 5, [ckv_sq[:, 0]])
            plain(S["fq"], x_hl, KT, first=1, last=2, ready=spread_q_kv)
            plain(S["fq"], x_hl, KT, first=2)
            plain(S["fk"], x_hl, KT)
            plain(S["fv"], x_hl, KT, values=True)
            pe.wait_ge(scaled, S["fk"].g0 + S["fk"].groups)
            attend(S["gates"], x_hl, KT, "fox")
            plain(S["gates"], x_hl, KT, first=8)
            pe.wait_ge(norm_split, KQ + KKV)
            plain(S["uq_nope"], cq_hl, KQ)
            plain(S["uq_rope"], cq_hl, KQ)
            plain(S["ukv_k"], ckv_hl, KKV)
            plain(S["ukv_v"], ckv_hl, KKV, values=True)
            pe.wait_ge(group_out, S["ukv_v"].g0 + 1)
            pe.wait_ge(o_split, HEADS // 2)
            attend(S["y_fox"], o_fox, HEADS, "mla")
            def mla_ready(ui):
                pe.wait_ge(o_split, HEADS // 2 + 2 * (ui + 1))
            plain(S["y_mla"], o_mla, HEADS, ready=mla_ready)

            def merged_ready(ui):
                pe.wait_ge(full_split, 2 * (ui + 1))
            plain(S["w_out"], m_hl, KT, ready=merged_ready)
            for i in range(MLP_PARTS):
                up = S[f"up{i}"]
                if i == 0:
                    plain(up, hn_hl, KT, last=1, ready=resid_ready)
                    plain(up, hn_hl, KT, first=1, last=2, ready=spread_mlp)
                    plain(up, hn_hl, KT, first=2)
                else:
                    plain(up, hn_hl, KT)
                def hidden_ready(ui, base=FULL0[f"up{i}"]):
                    pe.wait_ge(full_split, base + 2 * (ui + 1))
                down = S[f"down{i}"]
                tail = 2 if down is STAGES[-1] else 0
                plain(down, u_hl, D_FF // P // MLP_PARTS, last=down.groups - tail, ready=hidden_ready)
                plain(down, u_hl, D_FF // P // MLP_PARTS, first=down.groups - tail)
            last_norm_sum()
            spread(LAST_NORM, 5)

        @block.scalar
        def _(act):
            def unit_to_hi(n, slot):
                act.wait_ge(unit_loaded[slot], (n - slot) * (16 // RING) + 16)
                if not isinstance(n, int) or n >= RING:
                    units_free(n)
                nc.scalar.activation(hl[:, slot, :, 0], raw[:, slot], ACT.Copy).then_inc(unit_hi, 1)

            def units_free(n):
                act.wait_ge(halves_used, n * 2 - 2 * (RING - 1))

            def low_half(stage, g, j):
                b0 = pair_of(stage, j)
                act.wait_ge(halves_used, halves_until(stage, g))
                if stage.g0 + j >= 2:
                    act.wait_ge(group_out, g + (stage.g0 - 1))
                scale = {"fq": FOX_SCALE, "uq_nope": MLA_SCALE, "uq_rope": MLA_SCALE}.get(stage.name, 1.0)
                n = 1 if stage.name == "krff" else 2
                nc.scalar.activation(part[:, (stage.g0 + j) % 2, 0:n], bank[:, b0:b0 + n, T:], ACT.Copy,
                                     scale=scale).then_inc(group_low, 1)

            def root(norm, b, d):
                act.wait_ge(squares_summed, norm + 1)
                sums = bank[:, 6:8, 0] if norm == LAST_NORM else bank[:, b, T:T + TB]
                nc.scalar.activation(std_col[:, norm], sums, ACT.Sqrt, scale=1.0 / d,
                                     bias=cst[:, C_EPS:C_EPS + 1]).then_inc(std_done, 1)

            def square_resid(stage, g):
                act.wait_ge(resid_done, g + (RESID0[stage.name] + 1))
                nc.scalar.activation(sq[:], resid[:, bass.ds(2 * g, 2)], ACT.Square).then_inc(resid_squared, 1)

            def resid_gain(g, dst, gcol, done):
                for b in range(2):
                    nc.scalar.activation(dst(bass.ds(2 * g + b, 1)), resid[:, bass.ds(2 * g + b, 1)], ACT.Copy,
                                         scale=gain[:, bass.ds(2 * g + (gcol + b), 1)]).then_inc(done, 1)

            def norm_his(norm, kt, src, dst, gcol):
                for k in range(kt):
                    if k % 2 == 0:
                        act.wait_ge(normed, NORMED0[norm] + k // 2 + 1)
                    nc.scalar.activation(dst[:, k, 0], src[:, k], ACT.Copy,
                                         scale=gain[:, gcol + k:gcol + k + 1]).then_inc(norm_hi, 1)

            def sigmoids(g):
                nc.scalar.activation(gate[:, bass.ds(2 * g, 2)], gate[:, bass.ds(2 * g, 2)],
                                     ACT.Sigmoid).then_inc(gate_done, 1)

            def exps(i):
                act.wait_ge(max_ready, i + 1)
                for hh in range(2):
                    for q, piece in ((0, slice(0, 1)), (1, slice(1, 3))):
                        c = 2 * q + hh
                        nc.scalar.activation(prob[:, hh, piece], prob[:, hh, piece], ACT.Exp,
                                             bias=cols[:, 1, c:c + 1],
                                             accum_out=cols[:, 2, c:c + 1]).then_inc(exp_done, 1)

            def prob_t_copy(i):
                act.wait_ge(transposed, i + 1)
                nc.scalar.activation(prob_t[:], bank[:, 6:8, 0:3 * P].rearrange("p b (k q) -> p b k q", k=3),
                                     ACT.Copy).then_inc(prob_t_ready, 1)

            def out_hi(i):
                dst = o_fox if i < 4 else o_mla
                act.wait_ge(mixed, i + 1)
                h = 2 * (i % 4)
                nc.scalar.activation(dst[:, h:h + 2, 0], bank[:, 6].rearrange("p (h t) -> p h t", h=2),
                                     ACT.Copy).then_inc(o_hi, 1)

            def attention_step(step, pair0):
                if step == -1:
                    exps(pair0)
                elif step % 2 == 0:
                    prob_t_copy(pair0 + step // 2)
                    if step < 6:
                        exps(pair0 + step // 2 + 1)
                else:
                    out_hi(pair0 + step // 2)

            def value_hi(stage, g, j, dst):
                f = g + FULL0[stage.name]
                if stage.name != "y_mla":
                    act.wait_ge(relu_ready, f + (1 - FULL0["up0"]))
                    nc.scalar.activation(full[:, j % 2], relu[:], ACT.Square).then_inc(full_ready, 1)
                act.wait_ge(full_ready, f + 1)
                nc.scalar.activation(dst[:, bass.ds(2 * g, 2), 0], full[:, j % 2], ACT.Copy).then_inc(full_hi, 1)

            act.dma_start(gain[:], gains).then_inc(x_loaded[0], 16)

            def split(stage, g, j, k):
                if stage.name == "cq" and g == 1 and k == 3:
                    act.wait_ge(consts_in, 16)
                    root(X_NORM, 4, D)
                elif stage.name == "up0" and j == 1 and k == 2:
                    root(MLP_NORM, 4, D)
                unit_to_hi(*slots_of(stage, g, j)[k])
                if stage.name == "cq" and g == 0:
                    act.wait_ge(x_loaded[k], X_LOADED[k])
                    for i in range(4 * k, 4 * k + 4):
                        nc.scalar.activation(x_hl[:, i, 0], x_in[:, i], ACT.Copy,
                                             scale=gain[:, G_ATTN + i:G_ATTN + i + 1]).then_inc(x_hi, 1)
                    if k == 3:
                        act.dma_start(cst[:], consts).then_inc(consts_in, 16)

            def take(stage, g, j):
                name = stage.name
                if stage is not STAGES[-1] or j < stage.groups - 1:
                    low_half(stage, g, j)
                if name == "ckv":
                    act.wait_ge(scaled, S["krff"].g0)
                    nc.scalar.activation(cq_sq[:], cq_z[:], ACT.Square).then_inc(qkv_squared, 1)
                    nc.scalar.activation(ckv_sq[:], ckv_z[:], ACT.Square).then_inc(qkv_squared, 1)
                elif name == "fq" and g == 0:
                    root(Q_NORM, 4, Q_LORA)
                    root(KV_NORM, 5, KV_LORA)
                elif name == "fq" and g == 1:
                    norm_his(Q_NORM, KQ, cq_n, cq_hl, G_Q)
                elif name == "fq" and g == 2:
                    norm_his(KV_NORM, KKV, ckv_n, ckv_hl, G_KV)
                elif name == "fk" and g == 0:
                    act.wait_ge(ff_abs, 1)
                    nc.scalar.activation(ff_c[FF:], ff_b[FF:], ACT.Exp, scale=-1.0).then_inc(ff_exp, 1)
                    act.wait_ge(ff_exp, 1)
                    nc.scalar.activation(ff_b[FF:], ff_c[FF:], ACT.Ln,
                                         bias=cst[FF:, C_ONE:C_ONE + 1]).then_inc(ff_ln, 1)
                elif name == "fv" and j == stage.groups - 1:
                    attention_step(-1, 0)
                elif name == "gates" and j < 8:
                    attention_step(g, 0)
                elif name == "gates":
                    act.wait_ge(scaled, g + stage.g0)
                    sigmoids(g - 8)
                    if j > 8:
                        sigmoids(g - 1)
                elif name == "uq_nope" and g == 0:
                    act.wait_ge(scaled, S["gates"].g0 + S["gates"].groups)
                    sigmoids(S["gates"].groups - 1)
                elif name == "ukv_v" and g == stage.groups - 1:
                    attention_step(-1, 4)
                elif name == "y_fox":
                    attention_step(g, 4)
                elif name == "y_mla":
                    if j:
                        value_hi(stage, g - 1, j - 1, m_hl)
                    if j == stage.groups - 1:
                        value_hi(stage, g, j, m_hl)
                elif name == "w_out":
                    square_resid(stage, g)
                    resid_gain(g, lambda k: hn_hl[:, k, 0], G_MLP, resid_hi)
                elif name.startswith("up"):
                    value_hi(stage, g, j, u_hl)
                elif name == "down1":
                    if j < stage.groups - 1:
                        square_resid(stage, g)
                    else:
                        act.wait_ge(last_done, 2)
                    resid_gain(g, lambda k: final_gain[:, k], G_FINAL, gain_done)

            walk(act, split, take)
            root(LAST_NORM, 4, D)

        @block.vector
        def _(dve):
            steps = [0]

            def then_wait(ins):
                steps[0] += 1
                ins.then_inc(vec_step, 1)
                dve.wait_ge(vec_step, steps[0])

            def unit_to_lo(n, slot):
                dve.wait_ge(unit_hi, n + 1)
                nc.vector.tensor_tensor(hl[:, slot, :, 1], raw[:, slot], hl[:, slot, :, 0].bitcast(F32),
                                        ALU.subtract).then_inc(unit_split, 1)

            def high_half(stage, g, j):
                b0 = pair_of(stage, j)
                dve.wait_ge(group_low, g + (stage.g0 + 1))
                low, name = part[:, (stage.g0 + j) % 2], stage.name
                merging = {"y_fox": 0, "y_mla": S["y_fox"].groups}.get(name)
                if merging is not None and merging + j >= 2:
                    dve.wait_ge(pair_used, g + (merging - 1))
                two = bass.ds(2 * g, 2)
                dst = {"cq": lambda: cq_z[:, two], "ckv": lambda: ckv_z[:, two],
                       "krff": lambda: kr_z[:], "fq": lambda: fq[:, two], "fk": lambda: fk[:, two],
                       "fv": lambda: v_fox[:, :, bass.ds(COLS * g, COLS)], "gates": lambda: gate[:, two],
                       "uq_nope": lambda: qn[:, two], "uq_rope": lambda: qr_z[:, g],
                       "ukv_k": lambda: kn[:, two],
                       "ukv_v": lambda: v_mla[:, :, bass.ds(COLS * g, COLS)]}.get(name, lambda: zsum[:] if merging is None else pair_sum[:, j % 2])()
                high, total = bank[:, b0:b0 + 2, 0:T], zsum[:]
                if name == "krff":
                    high, low, total = bank[:, b0, 0:T], low[:, 0], zsum[:, 0]
                final_dst = dst
                if name in FROM_X:
                    dst = total
                if name in ("fq", "uq_nope", "uq_rope"):
                    scale = FOX_SCALE if name == "fq" else MLA_SCALE
                    ins = nc.vector.scalar_tensor_tensor(dst, high, scale, low, ALU.mult, ALU.add)
                else:
                    ins = nc.vector.tensor_tensor(dst, high, low, ALU.add)
                ins.then_inc(group_out, 1)
                if name not in FROM_X:
                    return
                summed(stage, g)
                if name == "fv":
                    for tb in range(TB):
                        ins = nc.vector.tensor_scalar(v_fox[:, tb, bass.ds(COLS * g, COLS)], zsum[:, tb],
                                                      rstd_col[:, X_NORM, tb:tb + 1], None, ALU.mult)
                elif name == "krff":
                    ins = nc.vector.tensor_tensor(final_dst, total, rstd[:, X_NORM], ALU.mult)
                else:
                    ins = nc.vector.tensor_tensor(final_dst, total, rstd_both(X_NORM), ALU.mult)
                ins.then_inc(scaled, 1)
                dve.wait_ge(scaled, g + (stage.g0 + 1))

            def rstd_both(norm):
                return rstd[:, norm].unsqueeze(1).broadcast_to([P, 2, T])

            def reciprocal_rms(norm):
                dve.wait_ge(std_done, norm + 1)
                nc.vector.reciprocal(rstd_col[:, norm], std_col[:, norm]).then_inc(rstd_col_done, 1)

            def take_rstd(norm):
                dve.wait_ge(rstd_spread, norm + 1)
                nc.vector.tensor_copy(rstd[:, norm], bank[:, 5 if norm == KV_NORM else 4, 0:T])\
                  .then_inc(rstd_ready, 1)
                dve.wait_ge(rstd_ready, norm + 1)

            def summed(stage, g):
                dve.wait_ge(group_out, g + (stage.g0 + 1))

            def norm(norm, kt, src, tmp, dst, gcol):
                take_rstd(norm)
                for j in range(kt // 2):
                    nc.vector.tensor_tensor(tmp[:, 2 * j:2 * j + 2], src[:, 2 * j:2 * j + 2], rstd_both(norm),
                                            ALU.mult).then_inc(normed, 1)
                dve.wait_ge(normed, NORMED0[norm] + kt // 2)
                for k in range(kt):
                    dve.wait_ge(norm_hi, SPLIT0[norm] + k + 1)
                    nc.vector.scalar_tensor_tensor(dst[:, k, 1], tmp[:, k], gain[:, gcol + k:gcol + k + 1],
                                                   dst[:, k, 0].bitcast(F32), ALU.mult,
                                                   ALU.subtract).then_inc(norm_split, 1)

            def sum_resid_squares(stage, g, i):
                n = g + (RESID0[stage.name] - (i * S["down0"].groups) + 1)
                dve.wait_ge(resid_squared, n)
                nc.vector.tensor_tensor(sq_sum[:, i], sq_sum[:, i], sq[:], ALU.add).then_inc(resid_summed, 1)
                dve.wait_ge(resid_summed, n)

            def swap_halves(dst, z, rows):
                for q in range(0, rows, 32):
                    ins = nc.vector.tensor_copy(dst[q:q + 32], z[q ^ 32:(q ^ 32) + 32])
                return ins

            def rotate_keys():
                r = slice(0, ROPE)
                then_wait(swap_halves(kr_swap, kr_z, ROPE))
                then_wait(nc.vector.tensor_tensor(kr_swap[r], kr_swap[r], cst[r, C_SIN:C_SIN + T], ALU.mult))
                then_wait(nc.vector.tensor_tensor(kr_z[r], kr_z[r], cst[r, C_COS:C_COS + T], ALU.mult))
                then_wait(nc.vector.tensor_tensor(k_rope[r, 0], kr_z[r], kr_swap[r], ALU.add))
                nc.vector.tensor_copy(k_rope[ROPE:, 1], k_rope[r, 0]).then_inc(rope_ready, 1)

            def forget_logits():
                f = slice(FF, P)
                then_wait(nc.vector.tensor_scalar(ff_a[f], kr_z[f], gain[f, G_FBIAS:G_FBIAS + 1], None, ALU.add))
                then_wait(nc.vector.scalar_tensor_tensor(ff_b[f], ff_a[f], -1.0, ff_a[f], ALU.mult, ALU.max))
                nc.vector.tensor_scalar(ff_a[f], ff_a[f], 0.0, None, ALU.min).then_inc(ff_abs, 1)
                dve.wait_ge(ff_abs, 1)

            def forget_sums():
                f = slice(FF, P)
                dve.wait_ge(ff_ln, 1)
                then_wait(nc.vector.tensor_tensor(ff_a[f], ff_a[f], ff_b[f], ALU.subtract))
                then_wait(nc.vector.tensor_tensor_scan(ff_c[f], cst[f, C_ONE:C_ONE + 1].broadcast_to([P - FF, T]), ff_a[f], 0.0,
                                                       ALU.mult, ALU.add))
                then_wait(nc.vector.tensor_copy(ff_hi[f], ff_c[f]))
                hi = ff_hi[f].bitcast(F32)
                nc.vector.tensor_tensor(ff_b[f], ff_c[f], hi, ALU.subtract)
                then_wait(nc.vector.tensor_scalar(ff_a[f], hi, cst[f, C_PART:C_PART + 1], None, ALU.mult))
                then_wait(nc.vector.scalar_tensor_tensor(ff_c[f], ff_b[f], cst[f, C_PART + 1:C_PART + 2], ff_a[f],
                                                         ALU.mult, ALU.add))
                then_wait(nc.vector.tensor_scalar(left[f], ff_c[f], cst[f, C_LEFT:C_LEFT + 1],
                                                  cst[f, C_LEFT + 1:C_LEFT + 2], ALU.mult, ALU.add))

            def bias_factor(i):
                f = slice(FF, P)
                if i:
                    dve.wait_ge(scored, i)
                for hh in range(2):
                    h = 2 * i + hh
                    ins = nc.vector.tensor_scalar(right[f, hh], ff_c[f], cst[f, C_RIGHT_M + h:C_RIGHT_M + h + 1],
                                                  cst[f, C_RIGHT_N + h:C_RIGHT_N + h + 1], ALU.mult, ALU.add)
                ins.then_inc(bias_ready, 1)

            def maxima(i):
                dve.wait_ge(scored, i + 1)
                c = C_MASK_FOX if i < 4 else C_MASK_MLA
                mask = cst[:, c:c + 3 * P].unsqueeze(1).broadcast_to([P, 2, 3 * P])
                then_wait(nc.vector.tensor_tensor(prob[:].rearrange("p h k q -> p h (k q)"), bank[:, 4:6, 0:3 * P],
                                                  mask, ALU.add))
                nc.vector.tensor_reduce(cols[:, 0, 0:2], prob[:, :, 0], AX.X, ALU.max)
                then_wait(nc.vector.tensor_reduce(cols[:, 0, 2:4], prob[:, :, 1:3].rearrange("p h k q -> p h (k q)"),
                                                  AX.X, ALU.max))
                nc.vector.tensor_scalar(cols[:, 1], cols[:, 0], -1.0, None, ALU.mult).then_inc(max_ready, 1)
                if i < 3:
                    bias_factor(i + 1)

            def normalize(i):
                dve.wait_ge(exp_done, 4 * (i + 1))
                then_wait(nc.vector.reciprocal(cols[:, 3], cols[:, 2]))
                for hh in range(2):
                    for q, piece in ((0, slice(0, 1)), (1, slice(1, 3))):
                        c = 2 * q + hh
                        ins = nc.vector.tensor_scalar(prob[:, hh, piece], prob[:, hh, piece],
                                                      cols[:, 3, c:c + 1], None, ALU.mult)
                ins.then_inc(prob_ready, 1)

            def out_lo(i):
                dst = o_fox if i < 4 else o_mla
                dve.wait_ge(o_hi, i + 1)
                h = 2 * (i % 4)
                nc.vector.tensor_tensor(dst[:, h:h + 2, 1], bank[:, 6].rearrange("p (h t) -> p h t", h=2),
                                        dst[:, h:h + 2, 0].bitcast(F32), ALU.subtract).then_inc(o_split, 1)

            def attention_step(step, pair0):
                if step == -1:
                    maxima(pair0)
                    normalize(pair0)
                elif step % 2 == 0:
                    if step < 6:
                        maxima(pair0 + step // 2 + 1)
                        normalize(pair0 + step // 2 + 1)
                else:
                    out_lo(pair0 + step // 2)

            def value_lo(stage, g, j, dst):
                f = g + FULL0[stage.name]
                dve.wait_ge(full_hi, f + 1)
                nc.vector.tensor_tensor(dst[:, bass.ds(2 * g, 2), 1], full[:, j % 2],
                                        dst[:, bass.ds(2 * g, 2), 0].bitcast(F32),
                                        ALU.subtract).then_inc(full_split, 1)

            def swap_queries(g):
                summed(S["uq_rope"], g)
                swap_halves(qr_swap[:, g], qr_z[:, g], P).then_inc(qr_swapped, 1)

            def add_resid(stage, g):
                summed(stage, g)
                two = bass.ds(2 * g, 2)
                nc.vector.tensor_tensor(resid[:, two], resid[:, two], zsum[:], ALU.add).then_inc(resid_done, 1)
                dve.wait_ge(resid_done, g + (RESID0[stage.name] + 1))
                if stage.name == "w_out":
                    for b in range(2):
                        one = bass.ds(2 * g + b, 1)
                        dve.wait_ge(resid_hi, g * 2 + (b + 1))
                        ins = nc.vector.scalar_tensor_tensor(
                            hn_hl[:, one, 1], resid[:, one], gain[:, bass.ds(2 * g + (G_MLP + b), 1)],
                            hn_hl[:, one, 0].bitcast(F32), ALU.mult, ALU.subtract)
                    ins.then_inc(resid_split, 1)
                    sum_resid_squares(stage, g, 0)
                elif stage.name == "down1":
                    sum_resid_squares(stage, g, 1)

            def last_resid(stage, g):
                b0 = pair_of(stage, g)
                for b in range(2):
                    k = 2 * g + b
                    dve.wait_ge(halves_used, 2 * N_UNITS - 1 + b)
                    then_wait(nc.vector.tensor_tensor(zsum[:, b], bank[:, b0 + b, 0:T], resid[:, k], ALU.add))
                    nc.vector.tensor_tensor(resid[:, k], zsum[:, b], bank[:, b0 + b, T:],
                                            ALU.add).then_inc(last_done, 1)
                    dve.wait_ge(last_done, b + 1)
                    nc.vector.tensor_tensor(sq[:, b], resid[:, k], resid[:, k], ALU.mult).then_inc(resid_summed, 1)

            def hidden(stage, g, j):
                summed(stage, g)
                f = g + FULL0[stage.name]
                nc.vector.scalar_tensor_tensor(relu[:], zsum[:], 0.0, rstd_both(MLP_NORM), ALU.max,
                                               ALU.mult).then_inc(relu_ready, 1)
                dve.wait_ge(relu_ready, f + (1 - FULL0["up0"]))
                value_lo(stage, g, j, u_hl)

            def split(stage, g, j, k):
                if stage.name == "cq" and g == 1 and k == 3:
                    reciprocal_rms(X_NORM)
                elif stage.name == "up0" and j == 1 and k == 2:
                    reciprocal_rms(MLP_NORM)
                unit_to_lo(*slots_of(stage, g, j)[k])
                if stage.name == "cq" and g == 0:
                    for i in range(4 * k, 4 * k + 4):
                        dve.wait_ge(x_hi, i + 1)
                        nc.vector.scalar_tensor_tensor(
                            x_hl[:, i, 1], x_in[:, i], gain[:, G_ATTN + i:G_ATTN + i + 1],
                            x_hl[:, i, 0].bitcast(F32), ALU.mult, ALU.subtract).then_inc(x_split, 1)
                elif stage.name == "cq" and k == 0:
                    dve.wait_ge(x_squared, 4)
                    then_wait(nc.vector.tensor_tensor(x_sq[:, 2], x_sq[:, 2], x_sq[:, 3], ALU.add))
                elif stage.name == "cq" and k == 1:
                    dve.wait_ge(x_squared, 5)
                    then_wait(nc.vector.tensor_tensor(x_sq[:, 0], x_sq[:, 0], x_sq[:, 2], ALU.add))
                    nc.vector.tensor_tensor(x_sq[:, 0, 0:2], x_sq[:, 0, 0:2], x_sq[:, 0, 2:4],
                                            ALU.add).then_inc(squares_ready, 1)

            def take(stage, g, j):
                name = stage.name
                if name == "cq" and g == 0:
                    take_rstd(X_NORM)
                elif name == "w_out" and j == 0:
                    dve.wait_ge(resid_in, 16)
                if stage is STAGES[-1] and j == stage.groups - 1:
                    last_resid(stage, g)
                    return
                high_half(stage, g, j)
                if name == "krff":
                    dve.wait_ge(consts_in, 16)
                    dve.wait_ge(zeroed, 4)
                    rotate_keys()
                elif name == "fq" and g == 0:
                    reciprocal_rms(Q_NORM)
                    reciprocal_rms(KV_NORM)
                elif name == "fq" and g == 1:
                    norm(Q_NORM, KQ, cq_z, cq_n, cq_hl, G_Q)
                elif name == "fq" and g == 2:
                    norm(KV_NORM, KKV, ckv_z, ckv_n, ckv_hl, G_KV)
                elif name == "fq" and g == 3:
                    forget_logits()
                elif name == "fk" and g == 1:
                    forget_sums()
                    bias_factor(0)
                elif name == "fv" and j == stage.groups - 1:
                    attention_step(-1, 0)
                elif name == "gates" and j < 8:
                    attention_step(g, 0)
                elif name == "uq_rope":
                    swap_queries(g)
                elif name == "ukv_v" and g == stage.groups - 1:
                    attention_step(-1, 4)
                elif name == "y_fox":
                    attention_step(g, 4)
                elif name == "y_mla":
                    if j:
                        value_lo(stage, g - 1, j - 1, m_hl)
                    if j == stage.groups - 1:
                        value_lo(stage, g, j, m_hl)
                elif name in RESID0:
                    add_resid(stage, g)
                elif name.startswith("up"):
                    if name == "up0" and j == 0:
                        take_rstd(MLP_NORM)
                    hidden(stage, g, j)

            walk(dve, split, take)
            reciprocal_rms(LAST_NORM)
            dve.wait_ge(rstd_spread, LAST_NORM + 1)
            for tiles in OUT_PIECES:
                dve.wait_ge(gain_done, tiles.stop)
                n = tiles.stop - tiles.start
                nc.vector.tensor_tensor(final[:, tiles], final_gain[:, tiles],
                                        bank[:, 5, 0:T].unsqueeze(1).broadcast_to([P, n, T]),
                                        ALU.mult).then_inc(final_done, 1)


def pack_stream(w_in, w_uq, w_ukv, w_mla_branch, w_fox_branch, w_out, w_up, w_down):
    stream = np.empty((N_UNITS, P, SLABS, COLS), w_in.dtype)
    at = [0]

    def columns(w, k_first=0, k_count=None):
        k_count = w.shape[0] // P if k_count is None else k_count
        w = w[k_first * P:(k_first + k_count) * P]
        groups = w.shape[1] // COLS
        units = (k_count // SLABS) * groups
        v = w.reshape(k_count // SLABS, SLABS, P, groups, COLS)
        stream[at[0]:at[0] + units] = v.transpose(3, 0, 2, 1, 4).reshape(units, P, SLABS, COLS)
        at[0] += units

    def half_units(w):
        v = w.reshape(2, P, w.shape[1] // COLS // 2, 2, COLS)
        units = w.shape[1] // COLS // 2
        stream[at[0]:at[0] + units] = v.transpose(2, 1, 3, 0, 4).reshape(units, P, SLABS, COLS)
        at[0] += units

    columns(w_in[:, 0:OFF_CKV])
    columns(w_in[:, OFF_CKV:OFF_KR])
    narrow = np.concatenate([w_in[:, OFF_KR:OFF_FQ]] + (P - FF) // HEADS * [w_in[:, OFF_FF:OFF_G]], axis=1)
    v = narrow.reshape(KT // SLABS // 2, SLABS, 2, P, P)
    stream[at[0]:at[0] + 2] = v.transpose(0, 3, 1, 2, 4).reshape(2, P, SLABS, COLS)
    at[0] += 2
    for first in (OFF_FQ, OFF_FK, OFF_FV):
        columns(w_in[:, first:first + HEADS * DH])
    columns(w_in[:, OFF_G:])
    uq = w_uq.reshape(Q_LORA, HEADS, DH + ROPE)
    columns(uq[:, :, :DH].reshape(Q_LORA, HEADS * DH))
    columns(uq[:, :, DH:].reshape(Q_LORA, HEADS * ROPE))
    ukv = w_ukv.reshape(KV_LORA, HEADS, 2, DH)
    half_units(ukv[:, :, 0].reshape(KV_LORA, HEADS * DH))
    half_units(ukv[:, :, 1].reshape(KV_LORA, HEADS * DH))
    columns(w_fox_branch)
    columns(w_mla_branch)
    columns(w_out)
    per = D_FF // MLP_PARTS
    for i in range(MLP_PARTS):
        columns(w_up[:, i * per:(i + 1) * per])
        columns(w_down, i * per // P, per // P)
    assert at[0] == N_UNITS
    return stream


def kernel(x, attn_norm, w_in, fox_f_bias, q_norm, w_uq, kv_norm, w_ukv,
           w_mla_branch, w_fox_branch, w_out, mlp_norm, w_up, w_down, final_norm):
    import concourse.bacc as bacc
    from concourse.bass_utils import run_bass_kernel_spmd

    a = np.asarray
    stream = pack_stream(a(w_in)[0], a(w_uq)[0], a(w_ukv)[0], a(w_mla_branch)[0], a(w_fox_branch)[0],
                         a(w_out)[0], a(w_up)[0], a(w_down)[0])
    x_t = np.ascontiguousarray(a(x)[0].T.reshape(KT, P, T).transpose(1, 0, 2))
    gains = np.zeros((P, G_COUNT), np.float32)
    for col, g in ((G_ATTN, a(attn_norm)[0]), (G_Q, a(q_norm)[0]), (G_KV, a(kv_norm)[0]),
                   (G_MLP, a(mlp_norm)[0]), (G_FINAL, a(final_norm))):
        gains[:, col:col + g.size // P] = g.reshape(-1, P).T
    for row in range(FF, P, HEADS):
        gains[row:row + HEADS, G_FBIAS] = a(fox_f_bias)[0]

    nc = bacc.Bacc("TRN2", target_bir_lowering=False, num_devices=1)
    arrays = {"weights": stream, "x_t": x_t, "consts": constants(), "gains": gains}
    aps = [nc.dram_tensor(k, v.shape, F32, kind="ExternalInput").ap() for k, v in arrays.items()]
    out_t = nc.dram_tensor("out_t", (P, KT, T), F32, kind="ExternalOutput").ap()
    program(nc, *aps, out_t)
    r = run_bass_kernel_spmd(nc, [arrays], core_ids=[0])
    y = r.results[0]["out_t"]
    return np.ascontiguousarray(y.transpose(1, 0, 2).reshape(D, T).T)[None]
```
